# Optimizing a Trainium2 kernel written in Bass

```python
import math
import jax, jax.numpy as jnp
from jax import lax
import numpy as np

D_MODEL = 1024
BATCH = 1
SEQ = 256
DEPTH = 2

CHUNK = 64
WINDOW = 128
WIN_CHUNKS = WINDOW // CHUNK
WIN_KEYS = WIN_CHUNKS * CHUNK
ATTN_WIDTH = D_MODEL // 2
POOL_WIDTH = D_MODEL - ATTN_WIDTH
HEAD_DIM = 64
N_Q_HEADS = ATTN_WIDTH // HEAD_DIM
N_KV_HEADS = 2
Q_PER_KV = N_Q_HEADS // N_KV_HEADS
KV_WIDTH = N_KV_HEADS * HEAD_DIM
POOL_WINDOWS = (2, 4, 8, 16)
N_POOL_GROUPS = len(POOL_WINDOWS)
POOL_GROUP_WIDTH = POOL_WIDTH // N_POOL_GROUPS
IN_WIDTH = ATTN_WIDTH + 2 * KV_WIDTH + POOL_WIDTH
D_FF = 2816
N_EXPERTS = 8
TOP_K = 2
N_DENSE = (DEPTH + 1) // 2
N_MOE = DEPTH // 2
RMS_EPS = 1e-6

kernel_name = "hybrid_swa_sink_pool_moe_sandwich"

def rms_norm(x, g):
    xf = x.astype(jnp.float32)
    y = xf * lax.rsqrt(jnp.mean(xf * xf, axis=-1, keepdims=True) + RMS_EPS)
    return (y * g.astype(jnp.float32)).astype(x.dtype)

def alibi_slopes(n_heads):
    h = jnp.arange(1, n_heads + 1, dtype=jnp.float32)
    return jnp.exp2(-8.0 * h / n_heads)

def window_attention(q, k, v, sinks):
    B, S = q.shape[0], q.shape[1]
    nc = S // CHUNK
    qb = q.reshape(B, nc, CHUNK, N_KV_HEADS, Q_PER_KV, HEAD_DIM)

    def windows(a):
        a = a.reshape(B, nc, CHUNK, N_KV_HEADS, HEAD_DIM)
        a = jnp.pad(a, ((0, 0), (WIN_CHUNKS - 1, 0), (0, 0), (0, 0), (0, 0)))
        return jnp.concatenate([a[:, j:j + nc] for j in range(WIN_CHUNKS)], axis=2)

    kw, vw = windows(k), windows(v)
    scores = jnp.einsum('bnqkgd,bnskd->bnkgqs', qb, kw).astype(jnp.float32) * (HEAD_DIM ** -0.5)
    qi = jnp.arange(CHUNK)
    kj = jnp.arange(WIN_KEYS)
    dist = jnp.abs(qi[:, None] + (WIN_CHUNKS - 1) * CHUNK - kj[None, :]).astype(jnp.float32)
    slopes = alibi_slopes(N_Q_HEADS).reshape(N_KV_HEADS, Q_PER_KV)
    scores = scores - slopes[:, :, None, None] * dist
    key_pos = (jnp.arange(nc)[:, None] - (WIN_CHUNKS - 1)) * CHUNK + kj[None, :]
    valid = key_pos >= 0
    scores = jnp.where(valid[None, :, None, None, None, :], scores, -jnp.inf)
    sink = jnp.broadcast_to(sinks.astype(jnp.float32).reshape(N_KV_HEADS, Q_PER_KV, 1, 1),
                            scores.shape[:-1] + (1,))
    probs = jax.nn.softmax(jnp.concatenate([scores, sink], axis=-1), axis=-1)[..., :-1]
    o = jnp.einsum('bnkgqs,bnskd->bnqkgd', probs.astype(vw.dtype), vw)
    return o.reshape(B, S, N_Q_HEADS * HEAD_DIM)

def multiscale_pool(u, pool_w, pool_scale):
    B, S, _ = u.shape
    uf = u.astype(jnp.float32)
    cs0 = jnp.pad(jnp.cumsum(uf, axis=1), ((0, 0), (1, 0), (0, 0)))
    pos = jnp.arange(1, S + 1, dtype=jnp.float32)
    outs = []
    for g, w in enumerate(POOL_WINDOWS):
        sl = slice(g * POOL_GROUP_WIDTH, (g + 1) * POOL_GROUP_WIDTH)
        hi = cs0[:, 1:, sl]
        lo = jnp.pad(cs0[:, :S + 1 - w, sl], ((0, 0), (w - 1, 0), (0, 0)))
        count = jnp.minimum(pos, float(w))[None, :, None]
        outs.append((hi - lo) / count - uf[:, :, sl])
    pooled = jnp.stack(outs, axis=2).astype(u.dtype)
    y = jnp.einsum('bsgc,gcd->bsgd', pooled, pool_w).reshape(B, S, POOL_WIDTH)
    return y * pool_scale

def swiglu(t, w_gate, w_up, w_down):
    return (jax.nn.silu(t @ w_gate) * (t @ w_up)) @ w_down

def moe_swiglu(h, w_router, w_gate, w_up, w_down):
    B, S, Dm = h.shape
    t = h.reshape(B * S, Dm)
    logits = (t @ w_router).astype(jnp.float32)
    top_vals, top_idx = lax.top_k(logits, TOP_K)
    top_w = jax.nn.softmax(top_vals, axis=-1)
    gates = jnp.sum(jax.nn.one_hot(top_idx, N_EXPERTS, dtype=jnp.float32) * top_w[..., None], axis=1)
    out = jnp.zeros((B * S, Dm), dtype=jnp.float32)
    for e in range(N_EXPERTS):
        ye = swiglu(t, w_gate[e], w_up[e], w_down[e]).astype(jnp.float32)
        out = out + gates[:, e:e + 1] * ye
    return out.astype(h.dtype).reshape(B, S, Dm)

def setup_inputs(seed: int = 0) -> dict:
    key = jax.random.key(seed)
    ks = jax.random.split(key, 20)
    f = jnp.float32

    def nrm(k, shape, fan_in):
        return jax.random.normal(k, shape, f) * (fan_in ** -0.5)

    def gain(k, shape):
        return 1.0 + 0.1 * jax.random.normal(k, shape, f)

    return {
        "x": jax.random.normal(ks[0], (BATCH, SEQ, D_MODEL), f),
        "pre_mix_gain": gain(ks[1], (DEPTH, D_MODEL)),
        "w_in": nrm(ks[2], (DEPTH, D_MODEL, IN_WIDTH), D_MODEL),
        "attn_sinks": jax.random.normal(ks[3], (DEPTH, N_Q_HEADS), f),
        "pool_w": nrm(ks[4], (DEPTH, N_POOL_GROUPS, POOL_GROUP_WIDTH, POOL_GROUP_WIDTH), POOL_GROUP_WIDTH),
        "pool_scale": gain(ks[5], (DEPTH, POOL_WIDTH)),
        "attn_out_gain": gain(ks[6], (DEPTH, ATTN_WIDTH)),
        "pool_out_gain": gain(ks[7], (DEPTH, POOL_WIDTH)),
        "w_out": nrm(ks[8], (DEPTH, D_MODEL, D_MODEL), D_MODEL),
        "post_mix_gain": gain(ks[9], (DEPTH, D_MODEL)),
        "pre_ffn_gain": gain(ks[10], (DEPTH, D_MODEL)),
        "post_ffn_gain": gain(ks[11], (DEPTH, D_MODEL)),
        "dense_w_gate": nrm(ks[12], (N_DENSE, D_MODEL, D_FF), D_MODEL),
        "dense_w_up": nrm(ks[13], (N_DENSE, D_MODEL, D_FF), D_MODEL),
        "dense_w_down": nrm(ks[14], (N_DENSE, D_FF, D_MODEL), D_FF),
        "moe_router": nrm(ks[15], (N_MOE, D_MODEL, N_EXPERTS), D_MODEL),
        "moe_w_gate": nrm(ks[16], (N_MOE, N_EXPERTS, D_MODEL, D_FF), D_MODEL),
        "moe_w_up": nrm(ks[17], (N_MOE, N_EXPERTS, D_MODEL, D_FF), D_MODEL),
        "moe_w_down": nrm(ks[18], (N_MOE, N_EXPERTS, D_FF, D_MODEL), D_FF),
    }

def reference(x, pre_mix_gain, w_in, attn_sinks, pool_w, pool_scale, attn_out_gain, pool_out_gain,
              w_out, post_mix_gain, pre_ffn_gain, post_ffn_gain, dense_w_gate, dense_w_up,
              dense_w_down, moe_router, moe_w_gate, moe_w_up, moe_w_down):
    B, S, _ = x.shape
    for l in range(DEPTH):
        h = rms_norm(x, pre_mix_gain[l])
        proj = h @ w_in[l]
        q = proj[..., :ATTN_WIDTH].reshape(B, S, N_Q_HEADS, HEAD_DIM)
        k = proj[..., ATTN_WIDTH:ATTN_WIDTH + KV_WIDTH].reshape(B, S, N_KV_HEADS, HEAD_DIM)
        v = proj[..., ATTN_WIDTH + KV_WIDTH:ATTN_WIDTH + 2 * KV_WIDTH].reshape(B, S, N_KV_HEADS, HEAD_DIM)
        u = proj[..., ATTN_WIDTH + 2 * KV_WIDTH:]
        ya = window_attention(q, k, v, attn_sinks[l])
        yp = multiscale_pool(u, pool_w[l], pool_scale[l])
        y = jnp.concatenate([rms_norm(ya, attn_out_gain[l]), rms_norm(yp, pool_out_gain[l])], axis=-1)
        y = y @ w_out[l]
        x = x + rms_norm(y, post_mix_gain[l])
        h = rms_norm(x, pre_ffn_gain[l])
        if l % 2 == 0:
            i = l // 2
            f_out = swiglu(h, dense_w_gate[i], dense_w_up[i], dense_w_down[i])
        else:
            i = l // 2
            f_out = moe_swiglu(h, moe_router[i], moe_w_gate[i], moe_w_up[i], moe_w_down[i])
        x = x + rms_norm(f_out, post_ffn_gain[l])
    return x


_drawn_inputs = setup_inputs


def setup_inputs(seed=0):
    import zlib

    import numpy as np

    out = dict(_drawn_inputs(seed))
    spreads = {}
    factors = {}
    for name, (base, spread) in spreads.items():
        noise = np.random.default_rng([zlib.crc32(name.encode()), seed]).standard_normal(out[name].shape)
        drawn = base * np.exp(spread * noise) if base else spread * noise
        out[name] = __import__('jax').numpy.asarray(drawn.astype(out[name].dtype))
    for name, factor in factors.items():
        out[name] = (out[name] * factor).astype(out[name].dtype)
    return out
```

```python
from contextlib import ExitStack

import concourse.bass as bass
from concourse import mybir

F32 = mybir.dt.float32
F32R = mybir.dt.float32r
I32 = mybir.dt.int32
ACT = mybir.ActivationFunctionType
ALU = mybir.AluOpType
AX = mybir.AxisListType

P = 128
EPS = 1e-6
CHUNK = 64
HEAD_DIM = 64
N_HEADS = 8
POOL_WINDOWS = (2, 4, 8, 16)
PAD = 16
FAR = 1e30
NOT_CHOSEN = -4096.0

PRE_MIX, POOL, ATTN, POST_MIX, PRE_FFN, POST_FFN = range(6)
T_MIX, T_OUT, T_FFN = range(3)
B_GU, B_TP, B_MISC, B_Y = 0, 2, 3, 4


def build_trunk(nc, x, pre_mix_gain, w_in, attn_sinks, pool_w, pool_scale, attn_out_gain, pool_out_gain, w_out,
                post_mix_gain, pre_ffn_gain, post_ffn_gain, dense_w_gate, dense_w_up, dense_w_down, moe_router,
                moe_w_gate, moe_w_up, moe_w_down, out):
    _, S, D = x.shape
    DEPTH = w_in.shape[0]
    E, _, F = moe_w_gate.shape[1:]
    KT = D // P
    TT = S // P
    FC = 256
    NCH = F // FC
    HALF = D // 2
    NG = len(POOL_WINDOWS)
    QM = HALF // P
    assert (S, D, TT, KT, DEPTH) == (256, 1024, 2, 8, 2) and NCH * FC == F and NCH % 2 == 1 and E % 2 == 0
    W_IN_USES, W_OUT_USES = 3, 2

    MIX_USES = W_IN_USES + W_OUT_USES

    def use_mix(l, n):
        return l * (MIX_USES + NCH) + n

    def use_ffn(l):
        return use_mix(l, MIX_USES)

    def norm_id(l, n, t):
        return TT * (6 * l + n) + t

    def tr_id(l, n, t):
        return TT * (3 * l + n) + t

    with ExitStack() as ctx:
        def sb(name, shape, dt=F32, at=ctx):
            return at.enter_context(nc.sbuf_tensor(name, shape, dt))

        def sem(name):
            return ctx.enter_context(nc.semaphore(name))

        raw_gu = sb("raw_gu", [P, 2, KT, 2 * FC])
        raw_d = sb("raw_d", [P, 2, 2, D])
        hi_gu = sb("hi_gu", [P, 2, KT, 2 * FC], F32R)
        lo_gu = sb("lo_gu", [P, 2, KT, 2 * FC], F32R)
        hi_d = sb("hi_d", [P, 2, D], F32R)
        lo_d = sb("lo_d", [P, 2, D], F32R)
        x_res = sb("x_res", [P, TT, D])
        rows = sb("rows", [P, TT, D])
        xt_hi = sb("xt_hi", [P, KT, S], F32R)
        xt_lo = sb("xt_lo", [P, KT, S], F32R)
        gains = [sb(f"gains{i}", [P, D]) for i in range(3)]
        pool_w_sb = sb("pool_w_sb", [P, NG, P])
        ident = sb("ident", [P, P])
        eps = sb("eps", [P, 1])
        sum_sq = sb("sum_sq", [P, 12 * TT])
        root = sb("root", [P, 12 * TT])
        rstd = sb("rstd", [P, 12 * TT])
        sinks = sb("sinks", [P, DEPTH, N_HEADS])
        recip_count = sb("recip_count", [P, NG, PAD])
        overflow = sb("overflow", [1, 2], I32)

        mix = ExitStack()
        dist = sb("dist", [P, 3 * P], at=mix)
        scores = sb("scores", [P, N_HEADS, S], at=mix)
        probs_t = sb("probs_t", [P, N_HEADS, TT, P], at=mix)
        q_t = sb("q_t", [P, QM, S], at=mix)
        k_t = sb("k_t", [P, 2, S], at=mix)
        v_rows = sb("v_rows", [P, TT, P], at=mix)
        u_t = sb("u_t", [P, NG, PAD + S], at=mix)
        junk = sb("junk", [P, HALF], at=mix)
        edge = sb("edge", [P, NG, PAD], at=mix)
        row_max = sb("row_max", [P, TT, N_HEADS], at=mix)
        top = sb("top", [P, TT, N_HEADS], at=mix)
        neg_top = sb("neg_top", [P, TT, N_HEADS], at=mix)
        denom = sb("denom", [P, TT, N_HEADS], at=mix)
        sink_gap = sb("sink_gap", [P, TT, N_HEADS], at=mix)
        sink_exp = sb("sink_exp", [P, TT, N_HEADS], at=mix)
        denom_all = sb("denom_all", [P, TT, N_HEADS], at=mix)
        inv_denom = sb("inv_denom", [P, TT, N_HEADS], at=mix)
        mix.close()
        sums = [scores[:].rearrange("p h s -> p (h s)")[:, 0:NG * (PAD + S)].rearrange("p (g s) -> p g s", g=NG),
                probs_t[:].rearrange("p h t s -> p (h t s)")[:, 0:NG * (PAD + S)].rearrange("p (g s) -> p g s", g=NG)]

        silu = sb("silu", [P, 2, FC])
        hidden = sb("hidden", [P, 2, FC])
        ht_hi = sb("ht_hi", [P, 2, S], F32R)
        ht_lo = sb("ht_lo", [P, 2, S], F32R)
        tok_hi = sb("tok_hi", [P, TT, D], F32R)
        tok_lo = sb("tok_lo", [P, TT, D], F32R)
        onehot = sb("onehot", [P, TT, P], F32R)
        onehot_t = sb("onehot_t", [P, S])
        slot_iota = sb("slot_iota", [P, P])
        router_raw = sb("router_raw", [P, KT, E])
        router_hi = sb("router_hi", [P, KT, E], F32R)
        router_lo = sb("router_lo", [P, KT, E], F32R)
        before = sb("before", [P, P])
        ones = sb("ones", [P, P])
        tie = sb("tie", [P, E, E])
        logits = sb("logits", [P, TT, E])
        beats = sb("beats", [P, E, E])
        ties = sb("ties", [P, E, E])
        rank = sb("rank", [P, TT, E])
        chosen = sb("chosen", [P, TT, E])
        best = sb("best", [P, TT])
        weight = sb("weight", [P, TT, E])
        weight_sum = sb("weight_sum", [P, TT])
        gates = sb("gates", [P, TT, E])
        slot = sb("slot", [P, 2, TT, E + 1])
        gap = sb("gap", [P, TT, E])
        most = sb("most", [1, 2])
        y_rows = gains[2]

        ps = ctx.enter_context(nc.psum_tensor("ps", [P, 8, 512], F32))

        def banks(b, n):
            return ps[:, b:b + n, :].rearrange("p b c -> p (b c)")

        x_loaded = sem("x_loaded")
        gu_loaded = [[sem(f"gu_loaded{b}_{h}") for h in range(2)] for b in range(2)]
        d_loaded = [sem(f"d_loaded{b}") for b in range(2)]
        gain_loaded = [sem(f"gain_loaded{i}") for i in range(3)]
        pool_w_loaded = sem("pool_w_loaded")
        sinks_loaded = sem("sinks_loaded")
        router_loaded = sem("router_loaded")
        gu_hi_done = sem("gu_hi_done")
        gu_lo_done = sem("gu_lo_done")
        gu_used = sem("gu_used")
        d_hi_done = sem("d_hi_done")
        d_lo_done = sem("d_lo_done")
        d_used = sem("d_used")
        const_made = sem("const_made")
        dist_made = sem("dist_made")
        masked = sem("masked")
        ffn_const_made = sem("ffn_const_made")
        sq_done = sem("sq_done")
        root_done = sem("root_done")
        rstd_done = sem("rstd_done")
        rows_ready = sem("rows_ready")
        tr_done = sem("tr_done")
        xt_hi_done = sem("xt_hi_done")
        xt_lo_done = sem("xt_lo_done")
        vec_step = sem("vec_step")
        x_updated = sem("x_updated")
        q_copied = sem("q_copied")
        kv_copied = sem("kv_copied")
        u_copied = sem("u_copied")
        pooled_ready = sem("pooled_ready")
        pool_mm = sem("pool_mm")
        pool_scaled = sem("pool_scaled")
        scores_mm = sem("scores_mm")
        scores_biased = sem("scores_biased")
        top_ready = sem("top_ready")
        gap_ready = sem("gap_ready")
        exp_done = sem("exp_done")
        sink_exp_done = sem("sink_exp_done")
        probs_turned = sem("probs_turned")
        probs_copied_a = sem("probs_copied_a")
        probs_copied_v = sem("probs_copied_v")
        attn_mm = sem("attn_mm")
        attn_scaled = sem("attn_scaled")
        gu_tile0 = sem("gu_tile0")
        silu_done = sem("silu_done")
        h_done = sem("h_done")
        h_turned = sem("h_turned")
        ht_hi_done = sem("ht_hi_done")
        ht_lo_done = sem("ht_lo_done")
        tok_hi_done = sem("tok_hi_done")
        tok_lo_done = sem("tok_lo_done")
        router_hi_done = sem("router_hi_done")
        router_lo_done = sem("router_lo_done")
        logits_mm = sem("logits_mm")
        gap_to_best = sem("gap_to_best")
        weight_exp = sem("weight_exp")
        experts_summed = sem("experts_summed")
        chosen_ready = sem("chosen_ready")
        rank_mm = sem("rank_mm")
        slots_ready = sem("slots_ready")
        onehot_ready = sem("onehot_ready")
        gathered_lo = sem("gathered_lo")
        gathered_hi = sem("gathered_hi")
        xg_hi_done = sem("xg_hi_done")
        xg_lo_done = sem("xg_lo_done")
        onehot_turned = sem("onehot_turned")
        onehot_t_copied = sem("onehot_t_copied")
        y_copied = sem("y_copied")
        scattered = sem("scattered")
        expert_added = sem("expert_added")
        out_stored = sem("out_stored")

        gain_plan = []
        for l in range(DEPTH):
            gain_plan += [(0, l, PRE_MIX), (1, l, ATTN), (2, l, POOL), (0, l, POST_MIX), (1, l, PRE_FFN),
                          (0 if l == DEPTH - 1 else 2, l, POST_FFN)]

        def gain_of(l, n):
            at = next(i for i, g in enumerate(gain_plan) if g[1:] == (l, n))
            s = gain_plan[at][0]
            return s, sum(g[0] == s for g in gain_plan[:at])

        GAIN_BYTES = {ATTN: 32, POOL: 16}

        def gain_level(s, fill):
            fills = [g for g in gain_plan if g[0] == s][:fill + 1]
            return sum(GAIN_BYTES.get(g[2], 16) for g in fills)

        def hidden_id(chunk, t, nt):
            return chunk * TT + t if nt == TT else chunk + (TT - 1) * NCH

        def ffn_steps(eng, first_use, first_chunk, step, tail):
            for c in (0, 1):
                step(c, first_use + c, first_chunk + c)
            with eng.Fori(0, (NCH - 3) // 2) as m:
                for c in (2, 3):
                    step(c, m * 2 + (first_use + c), m * 2 + (first_chunk + c), m)
            step(NCH - 1, first_use + NCH - 1, first_chunk + NCH - 1)
            tail(first_chunk + NCH - 1)

        block = ctx.enter_context(nc.Block())

        @block.sync
        def _(sp):
            def free_half(use, h):
                if not (isinstance(use, int) and use < 2):
                    sp.wait_ge(gu_lo_done, use * 2 + (h - 3))

            def load_mix(l, n):
                u = use_mix(l, n)
                w = w_in[l] if n < W_IN_USES else w_out[l]
                c0 = 2 * FC * (n if n < W_IN_USES else n - W_IN_USES)
                half = min(2 * FC, w.shape[1] - c0) // 2
                for h in range(2):
                    free_half(u, 1 if n == 4 else h)
                    sp.dma_start(raw_gu[:, u % 2, :, h * half:(h + 1) * half],
                                 w[:, c0 + h * half:c0 + (h + 1) * half].rearrange("(k p) n -> p k n", p=P)
                                 ).then_inc(gu_loaded[u % 2][h], 16)

            def load_gate_up(w_gate, w_up, use, parity, cols):
                for h, w in enumerate((w_gate, w_up)):
                    free_half(use, h)
                    sp.dma_start(raw_gu[:, parity, :, h * FC:(h + 1) * FC],
                                 w[:, cols].rearrange("(k p) n -> p k n", p=P)).then_inc(gu_loaded[parity][h], 16)

            def free_down(chunk):
                if not (isinstance(chunk, int) and chunk < 2):
                    sp.wait_ge(d_lo_done, chunk - 1)

            def load_down(w_down, rows_of_chunk, d_parity):
                sp.dma_start(raw_d[:, d_parity, :, :], w_down[rows_of_chunk, :].rearrange("(k p) n -> p k n", p=P)
                             ).then_inc(d_loaded[d_parity], 16)

            def load_network(w_gate, w_up, w_down, use0, parity0, chunk0, d_parity0, load_next):
                def gate_up(c, m=None):
                    c_at = c if m is None else m * 2 + c
                    load_gate_up(w_gate, w_up, use0 + c_at, (parity0 + c) % 2, bass.ds(c_at * FC, FC))

                def down(c, m=None):
                    c_at = c if m is None else m * 2 + c
                    if c:
                        free_down(chunk0 + c_at)
                    load_down(w_down, bass.ds(c_at * FC, FC), (d_parity0 + c) % 2)

                free_down(chunk0)
                gate_up(1)
                for c in (0, 1):
                    down(c)
                    gate_up(c + 2)
                with sp.Fori(0, (NCH - 5) // 2) as m:
                    for c in (2, 3):
                        down(c, m)
                        gate_up(c + 2, m)
                down(NCH - 3)
                gate_up(NCH - 1)
                down(NCH - 2)
                load_next()
                down(NCH - 1)

            def load_experts(n_pass):
                def pair(i, last):
                    for half in range(2):
                        e = i * 2 + half
                        use0 = i * (2 * NCH) + (use_ffn(1) + (n_pass * E + half) * NCH)
                        parity0 = (use_ffn(1) + half * NCH) % 2
                        pick = lambda w, n: w[0, bass.ds(n, 1)].rearrange("a k n -> (a k) n")
                        after = 0 if last and half == 1 else e + 1
                        load_next = lambda: load_gate_up(pick(moe_w_gate, after), pick(moe_w_up, after), use0 + NCH,
                                                         (parity0 + NCH) % 2, slice(0, FC))
                        load_network(pick(moe_w_gate, e), pick(moe_w_up, e), pick(moe_w_down, e), use0, parity0,
                                     i * (2 * NCH) + (n_pass * E + half + 1) * NCH, (half + 1) % 2, load_next)

                with sp.Fori(0, E // 2 - 1) as i:
                    pair(i, False)
                pair(E // 2 - 1, True)

            for n in range(MIX_USES):
                load_mix(0, n)
            u = use_ffn(0)
            load_gate_up(dense_w_gate[0], dense_w_up[0], u, u % 2, slice(0, FC))
            load_network(dense_w_gate[0], dense_w_up[0], dense_w_down[0], u, u % 2, 0, 0, lambda: load_mix(1, 0))
            for n in range(1, MIX_USES):
                load_mix(1, n)
            u = use_ffn(1)
            load_gate_up(moe_w_gate[0, 0], moe_w_up[0, 0], u, u % 2, slice(0, FC))
            load_experts(0)
            sp.wait_ge(slots_ready, 1)
            count = sp.value_load(overflow[0:1, 0:1], min_val=0, max_val=S)
            with sp.If(count > P):
                load_experts(1)
            for t in range(TT):
                sp.wait_ge(x_updated, TT * (2 * DEPTH - 1) + t + 1)
                sp.dma_start(out[0, t * P:(t + 1) * P, :], x_res[:, t, :]).then_inc(out_stored, 16)
            sp.wait_ge(out_stored, 16 * TT)

        @block.gpsimd
        def _(pool):
            pool.memset(ident[:], 0.0).then_inc(const_made, 1)
            pool.memset(eps[:], EPS).then_inc(const_made, 1)
            pool.wait_ge(const_made, 2)
            pool.affine_select(out=ident[:], in_=ident[:], compare_op=ALU.not_equal, fill=1.0, base=0,
                               pattern=[[-1, P]], channel_multiplier=1).then_inc(const_made, 1)
            pool.iota(recip_count[:], pattern=[[0, NG], [1, PAD]], base=1, channel_multiplier=0,
                      allow_small_or_imprecise_dtypes=True).then_inc(const_made, 1)
            pool.dma_start(sinks[:].rearrange("p l h -> p (l h)"),
                           attn_sinks.rearrange("(a l) h -> a (l h)", a=1).broadcast_to([P, DEPTH * N_HEADS])
                           ).then_inc(sinks_loaded, 16)

            def load_gain(n):
                s, l, what = gain_plan[n]
                fill = gain_of(l, what)[1]
                if fill:
                    _, lf, former = [g for g in gain_plan[:n] if g[0] == s][-1]
                    pool.wait_ge(*{PRE_MIX: (rows_ready, tr_id(lf, T_MIX, 1) + 1),
                                   POOL: (pool_scaled, TT * (lf + 1)),
                                   ATTN: (rows_ready, tr_id(lf, T_OUT, 1) + 1),
                                   POST_MIX: (x_updated, TT * (2 * lf + 1)),
                                   PRE_FFN: (rows_ready, tr_id(lf, T_FFN, 1) + 1),
                                   POST_FFN: (x_updated, TT * (2 * lf + 2))}[former])
                wide = lambda g: g[l:l + 1, :].broadcast_to([P, g.shape[1]])
                if what == ATTN:
                    pool.dma_start(gains[s][:, 0:HALF], wide(attn_out_gain)).then_inc(gain_loaded[s], 16)
                    pool.dma_start(gains[s][:, HALF:D], wide(pool_out_gain)).then_inc(gain_loaded[s], 16)
                elif what == POOL:
                    pool.dma_start(gains[s][:, 0:HALF], wide(pool_scale)).then_inc(gain_loaded[s], 16)
                else:
                    g = {PRE_MIX: pre_mix_gain, POST_MIX: post_mix_gain, PRE_FFN: pre_ffn_gain,
                         POST_FFN: post_ffn_gain}[what]
                    pool.dma_start(gains[s][:], wide(g)).then_inc(gain_loaded[s], 16)

            def make_dist():
                for t, c0, n in ((0, 0, P), (1, P, 2 * P)):
                    pool.iota(dist[:, c0:c0 + n], pattern=[[-1, n]], base=t * P, channel_multiplier=1,
                              allow_small_or_imprecise_dtypes=True).then_inc(dist_made, 1)

            def mask_dist(l):
                pool.wait_ge(dist_made, 3 * l + 3)
                hidden_keys = [dist[0:CHUNK, CHUNK:P],
                        dist[0:CHUNK, P:P + CHUNK], dist[0:CHUNK, P + 3 * CHUNK:P + 4 * CHUNK],
                        dist[CHUNK:P, P:P + 2 * CHUNK]]
                for s in hidden_keys:
                    pool.memset(s, FAR).then_inc(masked, 1)

            for n in range(3):
                load_gain(n)
            pool.dma_start(pool_w_sb[:], pool_w[0].rearrange("g c d -> c g d")).then_inc(pool_w_loaded, 16)
            make_dist()
            mask_dist(0)
            for n in range(3, 6):
                load_gain(n)
            pool.wait_ge(pool_mm, TT)
            pool.dma_start(pool_w_sb[:], pool_w[1].rearrange("g c d -> c g d")).then_inc(pool_w_loaded, 16)
            for n in range(6, 9):
                load_gain(n)
            pool.wait_ge(d_used, NCH)
            make_dist()
            mask_dist(1)
            for n in range(9, 12):
                load_gain(n)
            pool.wait_ge(rows_ready, tr_id(1, T_OUT, 1) + 1)
            pool.dma_start(router_raw[:], moe_router[0].rearrange("(k p) e -> p k e", p=P)
                           ).then_inc(router_loaded, 16)
            pool.iota(slot_iota[:], pattern=[[1, P]], base=0, channel_multiplier=0,
                      allow_small_or_imprecise_dtypes=True).then_inc(ffn_const_made, 1)
            pool.memset(ones[:], 1.0).then_inc(ffn_const_made, 1)
            pool.memset(before[:], 1.0).then_inc(ffn_const_made, 1)
            pool.memset(tie[:], 1.0).then_inc(ffn_const_made, 1)
            pool.memset(slot[:], NOT_CHOSEN).then_inc(ffn_const_made, 1)
            pool.wait_ge(ffn_const_made, 5)
            pool.affine_select(out=before[:], in_=before[:], compare_op=ALU.is_gt, fill=0.0, base=0,
                               pattern=[[1, P]], channel_multiplier=-1).then_inc(ffn_const_made, 1)
            pool.affine_select(out=tie[:], in_=tie[:], compare_op=ALU.is_gt, fill=0.0, base=0,
                               pattern=[[1, E], [-1, E]], channel_multiplier=0).then_inc(ffn_const_made, 1)

        @block.scalar
        def _(act):
            act.dma_start(x_res[:], x[0].rearrange("(t p) d -> p t d", p=P)).then_inc(x_loaded, 16)

            def split_gu(use, parity, h, level, width=2 * FC):
                act.wait_ge(gu_loaded[parity][h], level)
                if not (isinstance(use, int) and use < 2):
                    act.wait_ge(gu_used, use - 1)
                cols = slice(h * width // 2, (h + 1) * width // 2)
                act.copy(hi_gu[:, parity, :, cols], raw_gu[:, parity, :, cols]).then_inc(gu_hi_done, 1)

            def split_static(use):
                width = FC if use in (use_mix(0, 2), use_mix(1, 2)) else 2 * FC
                for h in range(2):
                    split_gu(use, use % 2, h, 16 * (use // 2 + 1), width)

            def norm(idx, src, junk_out, n):
                act.activation(junk_out, src, ACT.Square, accum_out=sum_sq[:, idx:idx + 1]).then_inc(sq_done, 1)
                act.wait_ge(sq_done, idx + 1)
                act.activation(root[:, idx:idx + 1], sum_sq[:, idx:idx + 1], ACT.Sqrt, scale=1.0 / n,
                               bias=eps[:, 0:1]).then_inc(root_done, 1)

            def transposed(l, n):
                for t in range(TT):
                    act.wait_ge(tr_done, tr_id(l, n, t) + 1)
                    act.copy(xt_hi[:, :, t * P:(t + 1) * P],
                             banks(B_Y + 2 * t, 2).rearrange("p (k s) -> p k s", k=KT)).then_inc(xt_hi_done, 1)

            def mixing(l):
                for t in range(TT):
                    if l:
                        act.wait_ge(x_updated, TT * (2 * l - 1) + t + 1)
                    else:
                        act.wait_ge(x_loaded, 16)
                    norm(norm_id(l, PRE_MIX, t), x_res[:, t, :], rows[:, t, :], D)
                if l == 0:
                    split_static(0)
                transposed(l, T_MIX)
                split_static(use_mix(l, 1))
                act.wait_ge(gu_used, use_mix(l, 0) + 1)
                act.copy(q_t[:], banks(B_Y, 2).rearrange("p (m s) -> p m s", m=QM)).then_inc(q_copied, 1)
                split_static(use_mix(l, 2))
                act.wait_ge(gu_used, use_mix(l, 1) + 1)
                for g in range(2):
                    for to in range(2):
                        act.copy(k_t[to * 64:(to + 1) * 64, g, :], ps[g * 64:(g + 1) * 64, 0, 0:S]
                                 ).then_inc(kv_copied, 1)
                act.copy(v_rows[:], ps[:, 1, 0:TT * P].rearrange("p (t c) -> p t c", t=TT)).then_inc(kv_copied, 1)
                act.copy(u_t[:, 0:2, PAD:PAD + S], ps[:, B_Y + 2, :].rearrange("p (g s) -> p g s", g=2)
                         ).then_inc(u_copied, 1)
                split_static(use_mix(l, 3))
                act.wait_ge(gu_used, use_mix(l, 2) + 1)
                act.copy(u_t[:, 2:4, PAD:PAD + S], ps[:, B_Y + 3, :].rearrange("p (g s) -> p g s", g=2)
                         ).then_inc(u_copied, 1)
                for t in range(TT):
                    if t:
                        split_static(use_mix(l, 4))
                    nk = (t + 1) * P
                    act.wait_ge(top_ready, TT * l + t + 1)
                    for s in range(N_HEADS):
                        act.activation(scores[:, s, 0:nk], scores[:, s, 0:nk], ACT.Exp,
                                       bias=neg_top[:, t, s:s + 1], scale=HEAD_DIM ** -0.5,
                                       accum_out=denom[:, t, s:s + 1]).then_inc(exp_done, 1)
                    act.wait_ge(gap_ready, TT * l + t + 1)
                    act.activation(sink_exp[:, t, :], sink_gap[:, t, :], ACT.Exp).then_inc(sink_exp_done, 1)
                    act.wait_ge(probs_turned, TT * l + t + 1)
                    b0 = (B_GU, B_Y)[t]
                    act.copy(probs_t[:, 0:4, 0:t + 1, :],
                             banks(b0, t + 1).rearrange("p (h k s) -> p h k s", h=4, k=t + 1)
                             ).then_inc(probs_copied_a, 1)
                for n in (POOL, ATTN):
                    for t in range(TT):
                        if n == POOL:
                            act.wait_ge(pool_scaled, TT * l + t + 1)
                        else:
                            act.wait_ge(attn_scaled, TT * l + t + 1)
                        c0 = HALF if n == POOL else 0
                        norm(norm_id(l, n, t), rows[:, t, c0:c0 + HALF], junk[:], HALF)
                transposed(l, T_OUT)
                for t in range(TT):
                    act.wait_ge(gu_used, use_mix(l, 4) + 1)
                    norm(norm_id(l, POST_MIX, t), banks(B_Y + 2 * t, 2), rows[:, t, :], D)
                split_static(use_ffn(l))
                for t in range(TT):
                    act.wait_ge(x_updated, TT * 2 * l + t + 1)
                    norm(norm_id(l, PRE_FFN, t), x_res[:, t, :], rows[:, t, :], D)
                transposed(l, T_FFN)

            def network(first_use, parity0, use_level, first_chunk, d_level, d_parity0, nt, after_first):
                def split_d(c, chunk, m):
                    b = (d_parity0 + c) % 2
                    act.wait_ge(d_loaded[b], (d_level(c) if m is None else d_level(c) + m * 16))
                    if not (isinstance(chunk, int) and chunk == 0):
                        act.wait_ge(d_used, chunk)
                    act.copy(hi_d[:], raw_d[:, b, :, :]).then_inc(d_hi_done, 1)

                def turn(chunk):
                    act.wait_ge(h_turned, chunk + 1)
                    w = nt * P
                    act.copy(ht_hi[:, :, 0:w], ps[:, B_TP, 0:2 * w].rearrange("p (k s) -> p k s", k=2)
                             ).then_inc(ht_hi_done, 1)

                def step(c, use, chunk, m=None):
                    if c > 0:
                        split_d(c - 1, chunk - 1, m)
                    nxt = (parity0 + c + 1) % 2
                    level = use_level(c + 1) if m is None else use_level(c + 1) + m * 16
                    split_gu(use + 1, nxt, 0, level)
                    if c > 0:
                        turn(chunk - 1)
                    if c == 1:
                        after_first()
                    split_gu(use + 1, nxt, 1, level)
                    for t in range(nt):
                        idx = hidden_id(chunk, t, nt)
                        b = t if nt == TT else (h_parity0 + c) % 2
                        if nt == TT and t == 0:
                            act.wait_ge(gu_tile0, chunk + 1)
                        else:
                            act.wait_ge(gu_used, use + 1)
                        if not (isinstance(idx, int) and idx < 2):
                            act.wait_ge(h_done, idx - 1)
                        act.activation(silu[:, b, :], ps[:, B_GU + b, 0:FC], ACT.Silu).then_inc(silu_done, 1)

                h_parity0 = (d_parity0 + NCH) % 2

                def tail(chunk):
                    split_d(NCH - 1, chunk, None)
                    turn(chunk)

                ffn_steps(act, first_use, first_chunk, step, tail)

            def experts(n_pass):
                def xg(gather, half):
                    act.wait_ge(gathered_hi, gather + 1)
                    act.copy(xt_hi[:, :, half * P:(half + 1) * P],
                             banks(B_Y + 2, 2).rearrange("p (k s) -> p k s", k=KT)).then_inc(xg_hi_done, 1)

                xg(n_pass * (E + 1), 0)
                base = n_pass * E
                with act.Fori(0, E // 2) as i:
                    for half in range(2):
                        e = i * 2 + (base + half)
                        use0 = use_ffn(1) + (base + half) * NCH
                        ch0 = NCH + (base + half) * NCH
                        use_lv = lambda c: i * (16 * NCH) + 16 * ((use0 + c) // 2 + 1)
                        d_lv = lambda c: i * (16 * NCH) + 16 * ((ch0 + c) // 2 + 1)
                        expert_network(i, e, use0, ch0, use_lv, d_lv)
                        act.wait_ge(d_used, i * (2 * NCH) + (ch0 + NCH))
                        act.copy(y_rows[:], banks(B_Y, 2)).then_inc(y_copied, 1)
                        xg(i * 2 + (n_pass * (E + 1) + half + 1), 1 - half)

            def expert_network(i, e, use0, ch0, use_lv, d_lv):
                def copy_onehot_t():
                    act.wait_ge(onehot_turned, e + 1)
                    act.copy(onehot_t[:], ps[:, B_Y + 2, 0:S]).then_inc(onehot_t_copied, 1)

                network(i * (2 * NCH) + use0, use0 % 2, use_lv, i * (2 * NCH) + ch0, d_lv, ch0 % 2, 1, copy_onehot_t)

            act.wait_ge(const_made, 4)
            for l in range(DEPTH):
                mixing(l)
                if l == 0:
                    network(use_ffn(0), use_ffn(0) % 2, lambda c: 16 * ((use_ffn(0) + c) // 2 + 1), 0,
                            lambda c: 16 * (c // 2 + 1), 0, TT, lambda: None)
                    for t in range(TT):
                        act.wait_ge(d_used, NCH)
                        norm(norm_id(0, POST_FFN, t), banks(B_Y + 2 * t, 2), rows[:, t, :], D)
            for t in range(TT):
                act.wait_ge(rows_ready, tr_id(1, T_FFN, t) + 1)
                act.copy(tok_hi[:, t, :], rows[:, t, :]).then_inc(tok_hi_done, 1)
            act.wait_ge(router_loaded, 16)
            act.copy(router_hi[:], router_raw[:]).then_inc(router_hi_done, 1)
            act.wait_ge(gap_to_best, 1)
            act.activation(weight[:], gap[:], ACT.Exp).then_inc(weight_exp, 1)
            experts(0)
            act.wait_ge(slots_ready, 1)
            count = act.value_load(overflow[0:1, 0:1], min_val=0, max_val=S)
            with act.If(count > P):
                experts(1)
            act.wait_ge(experts_summed, 1)
            for t in range(TT):
                norm(norm_id(1, POST_FFN, t), rows[:, t, :], y_rows[:], D)

        @block.tensor
        def _(pe):
            def mm3(o, a_hi, a_lo, b_hi, b_lo, first, last):
                pe.matmul(o, a_hi, b_hi, start=first, stop=False)
                pe.matmul(o, a_hi, b_lo, start=False, stop=False)
                return pe.matmul(o, a_lo, b_hi, start=False, stop=last)

            def turn_rows(l, n):
                for t in range(TT):
                    pe.wait_ge(rows_ready, tr_id(l, n, t) + 1)
                    for k in range(KT):
                        last = pe.transpose(ps[:, B_Y + 2 * t + k // 4, (k % 4) * P:(k % 4 + 1) * P],
                                            rows[:, t, k * P:(k + 1) * P], ident[:])
                    last.then_inc(tr_done, 1)
                pe.wait_ge(xt_lo_done, tr_id(l, n, TT - 1) + 1)

            def rows_times(use, b0):
                for t in range(TT):
                    for k in range(KT):
                        if t == 0 and k == 0:
                            pe.wait_ge(gu_lo_done, 2 * use + 2)
                        a = slice(t * P, (t + 1) * P)
                        last = mm3(ps[:, b0(t), :], xt_hi[:, k, a], xt_lo[:, k, a], hi_gu[:, use % 2, k, :],
                                   lo_gu[:, use % 2, k, :], k == 0, k == KT - 1)
                last.then_inc(gu_used, 1)

            def cols_times(use, c0, o):
                b = use % 2
                for k in range(KT):
                    last = mm3(o, hi_gu[:, b, k, c0:c0 + P], lo_gu[:, b, k, c0:c0 + P], xt_hi[:, k, :],
                               xt_lo[:, k, :], k == 0, k == KT - 1)
                return last

            def mixing(l):
                turn_rows(l, T_MIX)
                u = use_mix(l, 0)
                for m in range(QM):
                    if m % 2 == 0:
                        pe.wait_ge(gu_lo_done, 2 * u + m // 2 + 1)
                    last = cols_times(u, m * P, ps[:, B_Y + m // 2, (m % 2) * S:(m % 2 + 1) * S])
                last.then_inc(gu_used, 1)
                u += 1
                pe.wait_ge(gu_lo_done, 2 * u + 2)
                cols_times(u, 0, ps[:, 0, 0:S])
                for t in range(TT):
                    for k in range(KT):
                        a = slice(t * P, (t + 1) * P)
                        mm3(ps[:, 1, t * P:(t + 1) * P], xt_hi[:, k, a], xt_lo[:, k, a],
                            hi_gu[:, u % 2, k, P:2 * P], lo_gu[:, u % 2, k, P:2 * P], k == 0, k == KT - 1)
                for m in range(2):
                    last = cols_times(u, (2 + m) * P, ps[:, B_Y + 2, m * S:(m + 1) * S])
                last.then_inc(gu_used, 1)
                u += 1
                pe.wait_ge(gu_lo_done, 2 * u + 2)
                for m in range(2):
                    last = cols_times(u, m * P, ps[:, B_Y + 3, m * S:(m + 1) * S])
                last.then_inc(gu_used, 1)

                def score_products(t):
                    nk = (t + 1) * P
                    for h in range(N_HEADS):
                        r, m = h % 2, h // 2
                        rows64 = slice(r * 64, (r + 1) * 64)
                        c0 = (m % 2) * S
                        last = pe.matmul(ps[:, B_Y + 2 * r + m // 2, c0:c0 + nk],
                                         q_t[rows64, m, t * P:(t + 1) * P], k_t[rows64, h // 4, 0:nk],
                                         start=True, stop=True)
                    last.then_inc(scores_mm, 1)

                pe.wait_ge(q_copied, l + 1)
                pe.wait_ge(kv_copied, 5 * (l + 1))
                pe.wait_ge(u_copied, 2 * (l + 1))
                score_products(0)
                pe.wait_ge(pooled_ready, l + 1)
                pe.wait_ge(pool_w_loaded, 16 * (l + 1))
                for t in range(TT):
                    for g in range(NG):
                        last = pe.matmul(ps[:, B_MISC - t, g * P:(g + 1) * P],
                                         u_t[:, g, PAD + t * P:PAD + (t + 1) * P], pool_w_sb[:, g, :],
                                         start=True, stop=True)
                    last.then_inc(pool_mm, 1)
                pe.wait_ge(scores_biased, N_HEADS * (TT * l + 1))
                score_products(1)
                for t in range(TT):
                    pe.wait_ge(exp_done, N_HEADS * (TT * l + t + 1))
                    if t:
                        pe.wait_ge(scores_biased, N_HEADS * (TT * l + t + 1))
                    for s in range(N_HEADS):
                        for kt in range(t + 1):
                            n = s * (t + 1) + kt
                            last = pe.transpose(ps[:, (B_GU, B_Y)[t] + n // 4, (n % 4) * P:(n % 4 + 1) * P],
                                                scores[:, s, kt * P:(kt + 1) * P], ident[:])
                    last.then_inc(probs_turned, 1)
                    pe.wait_ge(pool_scaled, TT * (l + 1))
                    pe.wait_ge(probs_copied_a, TT * l + t + 1)
                    pe.wait_ge(probs_copied_v, TT * l + t + 1)
                    for h in range(N_HEADS):
                        s = (h % 2) * 4 + h // 2
                        kv = slice((h // 4) * HEAD_DIM, (h // 4 + 1) * HEAD_DIM)
                        for kt in range(t + 1):
                            last = pe.matmul(ps[:, B_TP + t, h * HEAD_DIM:(h + 1) * HEAD_DIM],
                                             probs_t[:, s, kt, :], v_rows[:, kt, kv], start=(kt == 0),
                                             stop=(kt == t))
                    last.then_inc(attn_mm, 1)
                turn_rows(l, T_OUT)
                for n in range(W_OUT_USES):
                    rows_times(use_mix(l, W_IN_USES + n), lambda t: B_Y + 2 * t + n)
                turn_rows(l, T_FFN)

            def network(first_use, parity0, first_chunk, h_parity0, nt, x0, before_first_turn, after_first_turn):
                def gate_up(c, use, chunk, t, before_second):
                    idx = hidden_id(chunk, t, nt)
                    b = t if nt == TT else (h_parity0 + c) % 2
                    w = (parity0 + c) % 2
                    if not (isinstance(idx, int) and idx < 2):
                        pe.wait_ge(h_done, idx - 1)
                    for k in range(KT):
                        if k == 0 and t == 0:
                            pe.wait_ge(gu_lo_done, use * 2 + 2)
                        if k == KT // 2:
                            before_second()
                        a = slice(x0 + t * P, x0 + (t + 1) * P)
                        last = mm3(ps[:, B_GU + b, :], xt_hi[:, k, a], xt_lo[:, k, a], hi_gu[:, w, k, :],
                                   lo_gu[:, w, k, :], k == 0, k == KT - 1)
                    last.then_inc(gu_tile0 if t < nt - 1 else gu_used, 1)

                def turn(c, chunk):
                    if c == 0:
                        before_first_turn()
                    pe.wait_ge(h_done, hidden_id(chunk, nt - 1, nt) + 1)
                    if not (isinstance(chunk, int) and chunk == 0):
                        pe.wait_ge(ht_lo_done, chunk)
                    for t in range(nt):
                        b = t if nt == TT else (h_parity0 + c) % 2
                        for k in range(2):
                            c0 = k * nt * P + t * P
                            last = pe.transpose(ps[:, B_TP, c0:c0 + P], hidden[:, b, k * P:(k + 1) * P], ident[:])
                    last.then_inc(h_turned, 1)
                    if c == 0:
                        after_first_turn()

                def down(c, chunk):
                    pe.wait_ge(ht_lo_done, chunk + 1)
                    pe.wait_ge(d_lo_done, chunk + 1)
                    for t in range(nt):
                        a = slice(t * P, (t + 1) * P)
                        for n in range(2):
                            cols = slice(n * 512, (n + 1) * 512)
                            for k in range(2):
                                last = mm3(ps[:, B_Y + 2 * t + n, :], ht_hi[:, k, a], ht_lo[:, k, a],
                                           hi_d[:, k, cols], lo_d[:, k, cols], c == 0 and k == 0,
                                           c == NCH - 1 and k == 1)
                    last.then_inc(d_used, 1)

                def step(c, use, chunk, m=None):
                    turn_prev = (lambda: turn(c - 1, chunk - 1)) if c else (lambda: None)
                    gate_up(c, use, chunk, 0, turn_prev)
                    if nt == TT:
                        gate_up(c, use, chunk, 1, lambda: None)
                    if c:
                        down(c - 1, chunk - 1)

                def tail(chunk):
                    turn(NCH - 1, chunk)
                    down(NCH - 1, chunk)

                ffn_steps(pe, first_use, first_chunk, step, tail)

            def gather(number):
                pe.wait_ge(onehot_ready, number + 1)
                for part, b0, done in ((tok_lo, B_TP, gathered_lo), (tok_hi, B_Y + 2, gathered_hi)):
                    for k in range(KT):
                        for t in range(TT):
                            last = pe.matmul(ps[:, b0 + k // 4, (k % 4) * P:(k % 4 + 1) * P],
                                             part[:, t, k * P:(k + 1) * P], onehot[:, t, :], start=(t == 0),
                                             stop=(t == TT - 1))
                    last.then_inc(done, 1)

            def experts(n_pass):
                base = n_pass * E
                g0 = n_pass * (E + 1)
                gather(g0)
                with pe.Fori(0, E // 2) as i:
                    for half in range(2):
                        e = i * 2 + (base + half)
                        pe.wait_ge(xg_hi_done, i * 2 + (g0 + half + 1))
                        pe.wait_ge(xg_lo_done, i * 2 + (g0 + half + 1))

                        def rows_added():
                            pe.wait_ge(expert_added, e * TT + 1)

                        def turn_onehot():
                            for t in range(TT):
                                last = pe.transpose(ps[:, B_Y + 2, t * P:(t + 1) * P],
                                                    onehot[:, t, :].bitcast(F32), ident[:])
                            last.then_inc(onehot_turned, 1)

                        use0 = use_ffn(1) + (base + half) * NCH
                        ch0 = NCH + (base + half) * NCH
                        network(i * (2 * NCH) + use0, use0 % 2, i * (2 * NCH) + ch0, (ch0 + NCH) % 2, 1, half * P,
                                rows_added, turn_onehot)
                        gather(i * 2 + (g0 + half + 1))
                        pe.wait_ge(y_copied, e + 1)
                        pe.wait_ge(onehot_t_copied, e + 1)
                        for t in range(TT):
                            if t == 0:
                                pe.wait_ge(xg_lo_done, i * 2 + (g0 + half + 2))
                            else:
                                pe.wait_ge(xg_hi_done, i * 2 + (g0 + half + 2))
                            for n in range(2):
                                last = pe.matmul(ps[:, (B_TP, B_Y + 2)[t] + n, :], onehot_t[:, t * P:(t + 1) * P],
                                                 y_rows[:, n * 512:(n + 1) * 512], start=True, stop=True)
                            last.then_inc(scattered, 1)

            pe.wait_ge(const_made, 4)
            for l in range(DEPTH):
                mixing(l)
                if l == 0:
                    network(use_ffn(0), use_ffn(0) % 2, 0, 0, TT, 0, lambda: None, lambda: None)
            pe.wait_ge(router_lo_done, 1)
            for t in range(TT):
                a = slice(t * P, (t + 1) * P)
                o = ps[:, B_MISC, t * E:(t + 1) * E]
                for k in range(KT):
                    mm3(o, xt_hi[:, k, a], xt_lo[:, k, a], router_hi[:, k, :], router_lo[:, k, :], k == 0, False)
                    last = pe.matmul(o, xt_lo[:, k, a], router_lo[:, k, :], start=False, stop=(k == KT - 1))
            last.then_inc(logits_mm, 1)
            pe.wait_ge(chosen_ready, 1)
            pe.wait_ge(ffn_const_made, 7)
            at = lambda n: ps[:, B_MISC, (4 + n) * E:(5 + n) * E]
            pe.matmul(at(0), before[:], chosen[:, 0, :], start=True, stop=True)
            pe.matmul(at(1), ones[:], chosen[:, 0, :], start=True, stop=False)
            pe.matmul(at(1), before[:], chosen[:, 1, :], start=False, stop=True)
            pe.matmul(at(2), ones[:], chosen[:, 0, :], start=True, stop=False)
            pe.matmul(at(2), ones[:], chosen[:, 1, :], start=False, stop=True).then_inc(rank_mm, 1)
            pe.wait_ge(tok_lo_done, TT)
            experts(0)
            pe.wait_ge(slots_ready, 1)
            count = pe.value_load(overflow[0:1, 0:1], min_val=0, max_val=S)
            with pe.If(count > P):
                experts(1)

        @block.vector
        def _(dve):
            steps = [0]

            def link(ins):
                steps[0] += 1
                ins.then_inc(vec_step, 1)
                dve.wait_ge(vec_step, steps[0])

            def split_gu(use, parity, p, width=2 * FC):
                dve.wait_ge(gu_hi_done, use * 2 + (p + 1))
                at = (slice(None), parity, slice(None), slice(p * width // 2, (p + 1) * width // 2))
                dve.tensor_tensor(lo_gu[at], raw_gu[at], hi_gu[at].bitcast(F32), ALU.subtract
                                  ).then_inc(gu_lo_done, 1)

            def split_static(use):
                width = FC if use in (use_mix(0, 2), use_mix(1, 2)) else 2 * FC
                for p in range(2):
                    split_gu(use, use % 2, p, width)

            def scale_of(idx):
                dve.wait_ge(root_done, idx + 1)
                dve.reciprocal(rstd[:, idx:idx + 1], root[:, idx:idx + 1]).then_inc(rstd_done, 1)
                dve.wait_ge(rstd_done, idx + 1)
                return rstd[:, idx:idx + 1]

            def low_parts(l, tr):
                for t in range(TT):
                    dve.wait_ge(xt_hi_done, tr_id(l, tr, t) + 1)
                    dve.tensor_tensor(xt_lo[:, :, t * P:(t + 1) * P],
                                      banks(B_Y + 2 * t, 2).rearrange("p (k s) -> p k s", k=KT),
                                      xt_hi[:, :, t * P:(t + 1) * P].bitcast(F32), ALU.subtract
                                      ).then_inc(xt_lo_done, 1)

            def pre_norm(l, n):
                s, fill = gain_of(l, n)
                for t in range(TT):
                    r = scale_of(norm_id(l, n, t))
                    dve.wait_ge(gain_loaded[s], gain_level(s, fill))
                    dve.scalar_tensor_tensor(rows[:, t, :], x_res[:, t, :], r, gains[s][:], ALU.mult, ALU.mult
                                             ).then_inc(rows_ready, 1)

            def post_norm(l, n, src):
                s, fill = gain_of(l, n)
                for t in range(TT):
                    r = scale_of(norm_id(l, n, t))
                    dve.wait_ge(gain_loaded[s], gain_level(s, fill))
                    link(dve.scalar_tensor_tensor(rows[:, t, :], src(t), r, gains[s][:], ALU.mult, ALU.mult))
                    dve.tensor_tensor(x_res[:, t, :], x_res[:, t, :], rows[:, t, :], ALU.add).then_inc(x_updated, 1)

            def pooling(l):
                link(dve.memset(u_t[:, :, 0:PAD], 0.0))
                dve.wait_ge(u_copied, 2 * (l + 1))
                a, b = sums
                W = PAD + S
                src, dst = u_t, a
                for g in range(NG):
                    w = 1 << g
                    lo = 2 * w - 1
                    link(dve.tensor_tensor(dst[:, g:NG, lo:W], src[:, g:NG, lo:W], src[:, g:NG, lo - w:W - w],
                                           ALU.add))
                    src, dst = dst, (b if dst is a else a)
                for g, w in enumerate(POOL_WINDOWS):
                    s = (a, b)[g % 2]
                    link(dve.tensor_tensor(edge[:, g, :], s[:, g, PAD:2 * PAD], recip_count[:, g, :], ALU.mult))
                    link(dve.tensor_tensor(u_t[:, g, PAD:2 * PAD], edge[:, g, :], u_t[:, g, PAD:2 * PAD],
                                           ALU.subtract))
                    last = dve.scalar_tensor_tensor(u_t[:, g, 2 * PAD:W], s[:, g, 2 * PAD:W], 1.0 / w,
                                                    u_t[:, g, 2 * PAD:W], ALU.mult, ALU.subtract)
                    if g < NG - 1:
                        link(last)
                last.then_inc(pooled_ready, 1)

            def attention_scores(l, t):
                nk = (t + 1) * P
                d0 = (0, P)[t]
                dve.wait_ge(scores_mm, TT * l + t + 1)
                dve.wait_ge(masked, 4 * (l + 1))
                dve.wait_ge(sinks_loaded, 16)
                if t:
                    dve.wait_ge(probs_turned, TT * l + t)
                for s in range(N_HEADS):
                    h = (s % 4) * 2 + s // 4
                    slope = 2.0 ** (-8.0 * (h + 1) / N_HEADS)
                    dve.scalar_tensor_tensor(scores[:, s, 0:nk], dist[:, d0:d0 + nk],
                                             -slope * HEAD_DIM ** 0.5,
                                             ps[:, B_Y + s // 2, (s % 2) * S:(s % 2) * S + nk],
                                             ALU.mult, ALU.add).then_inc(scores_biased, 1)
                dve.wait_ge(scores_biased, N_HEADS * (TT * l + t + 1))
                link(dve.tensor_reduce(row_max[:, t, :], scores[:, :, 0:nk], AX.X, ALU.max))
                sink = sinks[:, l, :].rearrange("p (m r) -> p r m", r=2)
                by = lambda x: x[:, t, :].rearrange("p (r m) -> p r m", r=2)
                link(dve.scalar_tensor_tensor(by(top), by(row_max), HEAD_DIM ** -0.5, sink, ALU.mult, ALU.max))
                dve.tensor_scalar(neg_top[:, t, :], top[:, t, :], -1.0, None, ALU.mult).then_inc(top_ready, 1)
                dve.tensor_tensor(by(sink_gap), sink, by(top), ALU.subtract).then_inc(gap_ready, 1)

            def attention_probs(l, t):
                dve.wait_ge(sink_exp_done, TT * l + t + 1)
                link(dve.tensor_tensor(denom_all[:, t, :], denom[:, t, :], sink_exp[:, t, :], ALU.add))
                link(dve.reciprocal(inv_denom[:, t, :], denom_all[:, t, :]))
                dve.wait_ge(probs_turned, TT * l + t + 1)
                b0 = (B_GU, B_Y)[t] + t + 1
                if t:
                    dve.wait_ge(attn_mm, TT * l + t)
                dve.tensor_copy(probs_t[:, 4:8, 0:t + 1, :],
                                banks(b0, t + 1).rearrange("p (h k s) -> p h k s", h=4, k=t + 1)
                                ).then_inc(probs_copied_v, 1)

            def attention_out(l, t):
                dve.wait_ge(attn_mm, TT * l + t + 1)
                dve.tensor_tensor(rows[:, t, 0:HALF].rearrange("p (m r d) -> p m r d", r=2, d=HEAD_DIM),
                                  ps[:, B_TP + t, :].rearrange("p (m r d) -> p m r d", r=2, d=HEAD_DIM),
                                  inv_denom[:, t, :].rearrange("p (r m a) -> p m r a", r=2, a=1)
                                  .broadcast_to([P, 4, 2, HEAD_DIM]), ALU.mult).then_inc(attn_scaled, 1)

            def mixing(l):
                pre_norm(l, PRE_MIX)
                if l == 0:
                    split_static(0)
                low_parts(l, T_MIX)
                dve.wait_ge(dist_made, 3 * l + 2)
                dve.scalar_tensor_tensor(dist[:], dist[:], -1.0, dist[:], ALU.mult, ALU.max).then_inc(dist_made, 1)
                for n in (1, 2, 3):
                    split_static(use_mix(l, n))
                pooling(l)
                attention_scores(l, 0)
                s, fill = gain_of(l, POOL)
                dve.wait_ge(gain_loaded[s], gain_level(s, fill))
                for t in range(TT):
                    dve.wait_ge(pool_mm, TT * l + t + 1)
                    dve.tensor_tensor(rows[:, t, HALF:D], ps[:, B_MISC - t, :], gains[s][:, 0:HALF], ALU.mult
                                      ).then_inc(pool_scaled, 1)
                attention_probs(l, 0)
                attention_scores(l, 1)
                attention_out(l, 0)
                split_static(use_mix(l, 4))
                attention_probs(l, 1)
                attention_out(l, 1)
                s, fill = gain_of(l, ATTN)
                dve.wait_ge(gain_loaded[s], gain_level(s, fill))
                for n, c0 in ((POOL, HALF), (ATTN, 0)):
                    for t in range(TT):
                        r = scale_of(norm_id(l, n, t))
                        ins = dve.scalar_tensor_tensor(rows[:, t, c0:c0 + HALF], rows[:, t, c0:c0 + HALF], r,
                                                       gains[s][:, c0:c0 + HALF], ALU.mult, ALU.mult)
                        if n == ATTN:
                            ins.then_inc(rows_ready, 1)
                        else:
                            link(ins)
                low_parts(l, T_OUT)
                post_norm(l, POST_MIX, lambda t: banks(B_Y + 2 * t, 2))
                split_static(use_ffn(l))
                pre_norm(l, PRE_FFN)
                low_parts(l, T_FFN)

            def network(first_use, parity0, first_chunk, d_parity0, nt):
                def split_d(c, chunk):
                    b = (d_parity0 + c) % 2
                    dve.wait_ge(d_hi_done, chunk + 1)
                    dve.tensor_tensor(lo_d[:], raw_d[:, b, :, :], hi_d[:].bitcast(F32), ALU.subtract
                                      ).then_inc(d_lo_done, 1)

                def turn(chunk):
                    w = nt * P
                    dve.wait_ge(ht_hi_done, chunk + 1)
                    dve.tensor_tensor(ht_lo[:, :, 0:w], ps[:, B_TP, 0:2 * w].rearrange("p (k s) -> p k s", k=2),
                                      ht_hi[:, :, 0:w].bitcast(F32), ALU.subtract).then_inc(ht_lo_done, 1)

                h_parity0 = (d_parity0 + NCH) % 2

                def step(c, use, chunk, m=None):
                    nxt = (parity0 + c + 1) % 2
                    if c > 0:
                        split_d(c - 1, chunk - 1)
                    split_gu(use + 1, nxt, 0)
                    if c > 0:
                        turn(chunk - 1)
                    split_gu(use + 1, nxt, 1)
                    for t in range(nt):
                        b = t if nt == TT else (h_parity0 + c) % 2
                        dve.wait_ge(silu_done, hidden_id(chunk, t, nt) + 1)
                        dve.tensor_tensor(hidden[:, b, :], silu[:, b, :], ps[:, B_GU + b, FC:2 * FC], ALU.mult
                                          ).then_inc(h_done, 1)

                def tail(chunk):
                    split_d(NCH - 1, chunk)
                    turn(chunk)

                ffn_steps(dve, first_use, first_chunk, step, tail)

            def choose():
                dve.wait_ge(logits_mm, 1)
                dve.wait_ge(ffn_const_made, 7)
                link(dve.tensor_copy(logits[:], ps[:, B_MISC, 0:TT * E].rearrange("p (t e) -> p t e", t=TT)))
                link(dve.tensor_reduce(best[:], logits[:], AX.X, ALU.max))
                wide = lambda x: x[:].rearrange("p (t a) -> p t a", a=1).broadcast_to([P, TT, E])
                dve.tensor_tensor(gap[:], logits[:], wide(best), ALU.subtract).then_inc(gap_to_best, 1)
                for t in range(TT):
                    other = logits[:, t, :].rearrange("p (a e) -> p a e", a=1).broadcast_to([P, E, E])
                    own = logits[:, t, :].rearrange("p (e a) -> p e a", a=1).broadcast_to([P, E, E])
                    link(dve.tensor_tensor(beats[:], other, own, ALU.is_gt))
                    link(dve.tensor_tensor(ties[:], other, own, ALU.is_equal))
                    link(dve.tensor_tensor(ties[:], ties[:], tie[:], ALU.mult))
                    link(dve.tensor_tensor(beats[:], beats[:], ties[:], ALU.add))
                    link(dve.tensor_reduce(rank[:, t, :], beats[:], AX.X, ALU.add))
                dve.tensor_scalar(chosen[:], rank[:], 1.5, None, ALU.is_lt).then_inc(chosen_ready, 1)
                dve.wait_ge(chosen_ready, 1)
                dve.wait_ge(weight_exp, 1)
                link(dve.tensor_tensor(weight[:], weight[:], chosen[:], ALU.mult))
                link(dve.tensor_reduce(weight_sum[:], weight[:], AX.X, ALU.add))
                link(dve.reciprocal(best[:], weight_sum[:]))
                link(dve.tensor_tensor(gates[:], weight[:], wide(best), ALU.mult))
                dve.wait_ge(rank_mm, 1)
                link(dve.scalar_tensor_tensor(rank[:], ps[:, B_MISC, 4 * E:6 * E].rearrange("p (t e) -> p t e", t=TT),
                                              -NOT_CHOSEN, chosen[:], ALU.add, ALU.mult))
                link(dve.tensor_scalar(slot[:, 0, :, 0:E], rank[:], NOT_CHOSEN, None, ALU.add))
                link(dve.tensor_scalar(slot[:, 1, :, 0:E], slot[:, 0, :, 0:E], -float(P), None, ALU.add))
                link(dve.tensor_reduce(most[0:1, 0:1], ps[0:1, B_MISC, 6 * E:7 * E], AX.X, ALU.max))
                dve.tensor_copy(overflow[0:1, 0:1], most[0:1, 0:1]).then_inc(slots_ready, 1)
                dve.wait_ge(slots_ready, 1)

            def experts(n_pass):
                base = n_pass * E
                g0 = n_pass * (E + 1)

                def make_onehot(number, expert):
                    for t in range(TT):
                        last = dve.tensor_scalar(onehot[:, t, :], slot_iota[:], slot[:, n_pass, t, expert], None,
                                                 ALU.is_equal)
                    last.then_inc(onehot_ready, 1)

                def gathered(number, half):
                    dve.wait_ge(gathered_lo, number + 1)
                    dve.tensor_copy(xt_lo[:, :, half * P:(half + 1) * P],
                                    banks(B_TP, 2).rearrange("p (k s) -> p k s", k=KT)).then_inc(xg_lo_done, 1)

                if n_pass:
                    dve.wait_ge(gathered_hi, g0)
                make_onehot(g0, slice(0, 1))
                gathered(g0, 0)
                with dve.Fori(0, E // 2) as i:
                    for half in range(2):
                        e = i * 2 + (base + half)
                        use0 = use_ffn(1) + (base + half) * NCH
                        ch0 = NCH + (base + half) * NCH
                        network(i * (2 * NCH) + use0, use0 % 2, i * (2 * NCH) + ch0, ch0 % 2, 1)
                        dve.wait_ge(onehot_turned, e + 1)
                        make_onehot(i * 2 + (g0 + half + 1), bass.ds(i * 2 + (half + 1), 1))
                        gathered(i * 2 + (g0 + half + 1), 1 - half)
                        for t in range(TT):
                            dve.wait_ge(scattered, e * TT + (t + 1))
                            dve.wait_ge(expert_added, e * TT + 1)
                            dve.scalar_tensor_tensor(rows[:, t, :], banks((B_TP, B_Y + 2)[t], 2),
                                                     gates[:, t, bass.ds(i * 2 + half, 1)], rows[:, t, :],
                                                     ALU.mult, ALU.add).then_inc(expert_added, 1)
                dve.wait_ge(expert_added, TT * (base + E) + 1)

            dve.wait_ge(const_made, 4)
            for g, w in enumerate(POOL_WINDOWS):
                link(dve.tensor_scalar(recip_count[:, g, :], recip_count[:, g, :], float(w), None, ALU.min))
            link(dve.reciprocal(recip_count[:], recip_count[:]))
            for l in range(DEPTH):
                mixing(l)
                if l == 0:
                    network(use_ffn(0), use_ffn(0) % 2, 0, 0, TT)
                    post_norm(0, POST_FFN, lambda t: banks(B_Y + 2 * t, 2))
            dve.wait_ge(router_hi_done, 1)
            dve.tensor_tensor(router_lo[:], router_raw[:], router_hi[:].bitcast(F32), ALU.subtract
                              ).then_inc(router_lo_done, 1)
            for t in range(TT):
                dve.wait_ge(tok_hi_done, t + 1)
                dve.tensor_tensor(tok_lo[:, t, :], rows[:, t, :], tok_hi[:, t, :].bitcast(F32), ALU.subtract
                                  ).then_inc(tok_lo_done, 1)
            choose()
            dve.wait_ge(tok_lo_done, TT)
            dve.memset(rows[:], 0.0).then_inc(expert_added, 1)
            experts(0)
            count = dve.value_load(overflow[0:1, 0:1], min_val=0, max_val=S)
            with dve.If(count > P):
                experts(1)
            dve.memset(most[0:1, 1:2], 0.0).then_inc(experts_summed, 1)
            post_norm(1, POST_FFN, lambda t: rows[:, t, :])


_INS = ["x", "pre_mix_gain", "w_in", "attn_sinks", "pool_w", "pool_scale", "attn_out_gain", "pool_out_gain", "w_out",
        "post_mix_gain", "pre_ffn_gain", "post_ffn_gain", "dense_w_gate", "dense_w_up", "dense_w_down",
        "moe_router", "moe_w_gate", "moe_w_up", "moe_w_down"]


def kernel(**inputs):
    import numpy as np
    import concourse.bacc as bacc
    from concourse.bass_utils import run_bass_kernel_spmd

    nc = bacc.Bacc("TRN2", target_bir_lowering=False, num_devices=1)
    arrays, args = {}, []
    for name in _INS:
        a = np.ascontiguousarray(inputs[name])
        arrays[f"in_{name}"] = a
        args.append(nc.dram_tensor(f"in_{name}", a.shape, mybir.dt.from_np(a.dtype), kind="ExternalInput").ap())
    out = nc.dram_tensor("out_0", arrays["in_x"].shape, F32, kind="ExternalOutput").ap()
    build_trunk(nc, *args, out)
    r = run_bass_kernel_spmd(nc, [arrays], core_ids=[0])
    return r.results[0]["out_0"]
```

```python
from contextlib import ExitStack

import concourse.bass as bass
from concourse import mybir

F32 = mybir.dt.float32
F32R = mybir.dt.float32r
I32 = mybir.dt.int32
ACT = mybir.ActivationFunctionType
ALU = mybir.AluOpType
AX = mybir.AxisListType

P = 128
EPS = 1e-6
CHUNK = 64
HEAD_DIM = 64
N_HEADS = 8
POOL_WINDOWS = (2, 4, 8, 16)
PAD = 16
FAR = 1e30
NOT_CHOSEN = -4096.0

PRE_MIX, POOL, ATTN, POST_MIX, PRE_FFN, POST_FFN = range(6)
T_MIX, T_OUT, T_FFN = range(3)
B_GU, B_TP, B_MISC, B_Y = 0, 2, 3, 4


def build_trunk(nc, x, pre_mix_gain, w_in, attn_sinks, pool_w, pool_scale, attn_out_gain, pool_out_gain, w_out,
                post_mix_gain, pre_ffn_gain, post_ffn_gain, dense_w_gate, dense_w_up, dense_w_down, moe_router,
                moe_w_gate, moe_w_up, moe_w_down, out):
    _, S, D = x.shape
    DEPTH = w_in.shape[0]
    E, _, F = moe_w_gate.shape[1:]
    KT = D // P
    TT = S // P
    FC = 256
    NCH = F // FC
    HALF = D // 2
    NG = len(POOL_WINDOWS)
    QM = HALF // P
    assert (S, D, TT, KT, DEPTH) == (256, 1024, 2, 8, 2) and NCH * FC == F and NCH % 2 == 1 and E % 2 == 0
    W_IN_USES, W_OUT_USES = 3, 2

    MIX_USES = W_IN_USES + W_OUT_USES

    def use_mix(l, n):
        return l * (MIX_USES + NCH) + n

    def use_ffn(l):
        return use_mix(l, MIX_USES)

    def norm_id(l, n, t):
        return TT * (6 * l + n) + t

    def tr_id(l, n, t):
        return TT * (3 * l + n) + t

    with ExitStack() as ctx:
        def sb(name, shape, dt=F32, at=ctx):
            return at.enter_context(nc.sbuf_tensor(name, shape, dt))

        def sem(name):
            return ctx.enter_context(nc.semaphore(name))

        raw_gu = sb("raw_gu", [P, 2, KT, 2 * FC])
        raw_d = sb("raw_d", [P, 2, 2, D])
        hi_gu = sb("hi_gu", [P, 2, KT, 2 * FC], F32R)
        lo_gu = sb("lo_gu", [P, 2, KT, 2 * FC], F32R)
        hi_d = sb("hi_d", [P, 2, D], F32R)
        lo_d = sb("lo_d", [P, 2, D], F32R)
        x_res = sb("x_res", [P, TT, D])
        rows = sb("rows", [P, TT, D])
        xt_hi = sb("xt_hi", [P, KT, S], F32R)
        xt_lo = sb("xt_lo", [P, KT, S], F32R)
        gains = [sb(f"gains{i}", [P, D]) for i in range(3)]
        pool_w_sb = sb("pool_w_sb", [P, NG, P])
        ident = sb("ident", [P, P])
        eps = sb("eps", [P, 1])
        sum_sq = sb("sum_sq", [P, 12 * TT])
        root = sb("root", [P, 12 * TT])
        rstd = sb("rstd", [P, 12 * TT])
        sinks = sb("sinks", [P, DEPTH, N_HEADS])
        recip_count = sb("recip_count", [P, NG, PAD])
        overflow = sb("overflow", [1, 2], I32)

        mix = ExitStack()
        dist = sb("dist", [P, 3 * P], at=mix)
        scores = sb("scores", [P, N_HEADS, S], at=mix)
        probs_t = sb("probs_t", [P, N_HEADS, TT, P], at=mix)
        q_t = sb("q_t", [P, QM, S], at=mix)
        k_t = sb("k_t", [P, 2, S], at=mix)
        v_rows = sb("v_rows", [P, TT, P], at=mix)
        u_t = sb("u_t", [P, NG, PAD + S], at=mix)
        junk = sb("junk", [P, HALF], at=mix)
        edge = sb("edge", [P, NG, PAD], at=mix)
        row_max = sb("row_max", [P, TT, N_HEADS], at=mix)
        top = sb("top", [P, TT, N_HEADS], at=mix)
        neg_top = sb("neg_top", [P, TT, N_HEADS], at=mix)
        denom = sb("denom", [P, TT, N_HEADS], at=mix)
        sink_gap = sb("sink_gap", [P, TT, N_HEADS], at=mix)
        sink_exp = sb("sink_exp", [P, TT, N_HEADS], at=mix)
        denom_all = sb("denom_all", [P, TT, N_HEADS], at=mix)
        inv_denom = sb("inv_denom", [P, TT, N_HEADS], at=mix)
        mix.close()
        sums = [scores[:].rearrange("p h s -> p (h s)")[:, 0:NG * (PAD + S)].rearrange("p (g s) -> p g s", g=NG),
                probs_t[:].rearrange("p h t s -> p (h t s)")[:, 0:NG * (PAD + S)].rearrange("p (g s) -> p g s", g=NG)]

        silu = sb("silu", [P, 2, FC])
        hidden = sb("hidden", [P, 2, FC])
        ht_hi = sb("ht_hi", [P, 2, S], F32R)
        ht_lo = sb("ht_lo", [P, 2, S], F32R)
        tok_hi = sb("tok_hi", [P, TT, D], F32R)
        tok_lo = sb("tok_lo", [P, TT, D], F32R)
        onehot = sb("onehot", [P, TT, P], F32R)
        onehot_t = sb("onehot_t", [P, S], F32R)
        slot_iota = sb("slot_iota", [P, P])
        router_raw = sb("router_raw", [P, KT, E])
        router_hi = sb("router_hi", [P, KT, E], F32R)
        router_lo = sb("router_lo", [P, KT, E], F32R)
        before = sb("before", [P, P])
        ones = sb("ones", [P, P])
        tie = sb("tie", [P, E, E])
        logits = sb("logits", [P, TT, E])
        logits_t = sb("logits_t", [E, S])
        beats = sb("beats", [P, E, E])
        ties = sb("ties", [P, E, E])
        rank = sb("rank", [P, TT, E])
        chosen = sb("chosen", [P, TT, E])
        best = sb("best", [P, TT])
        weight = sb("weight", [P, TT, E])
        weight_sum = sb("weight_sum", [P, TT])
        gates = sb("gates", [P, TT, E])
        slot = sb("slot", [P, 2, TT, E + 1])
        gap = sb("gap", [P, TT, E])
        most = sb("most", [1, 2])

        picked = gains[1]

        def y_part(xt, half):
            return xt[:, :, half * P:(half + 1) * P]

        ps = ctx.enter_context(nc.psum_tensor("ps", [P, 8, 512], F32))

        def banks(b, n):
            return ps[:, b:b + n, :].rearrange("p b c -> p (b c)")

        x_loaded = [sem(f"x_loaded{t}") for t in range(TT)]
        gu_loaded = [[sem(f"gu_loaded{b}_{h}") for h in range(2)] for b in range(2)]
        d_loaded = [sem(f"d_loaded{b}") for b in range(2)]
        gain_loaded = [sem(f"gain_loaded{i}") for i in range(3)]
        pool_w_loaded = sem("pool_w_loaded")
        sinks_loaded = sem("sinks_loaded")
        router_loaded = sem("router_loaded")
        gu_hi_done = sem("gu_hi_done")
        gu_lo_done = sem("gu_lo_done")
        gu_used = sem("gu_used")
        d_hi_done = sem("d_hi_done")
        d_lo_done = sem("d_lo_done")
        d_used = sem("d_used")
        const_made = sem("const_made")
        dist_made = sem("dist_made")
        masked = sem("masked")
        ffn_const_made = sem("ffn_const_made")
        sq_done = sem("sq_done")
        root_done = sem("root_done")
        rstd_done = sem("rstd_done")
        rows_ready = sem("rows_ready")
        tr_done = sem("tr_done")
        xt_hi_done = sem("xt_hi_done")
        xt_lo_done = sem("xt_lo_done")
        vec_step = sem("vec_step")
        x_updated = sem("x_updated")
        q_copied = sem("q_copied")
        kv_copied = sem("kv_copied")
        u_copied = sem("u_copied")
        pooled_ready = sem("pooled_ready")
        pool_mm = sem("pool_mm")
        pool_scaled = sem("pool_scaled")
        scores_mm = sem("scores_mm")
        scores_biased = sem("scores_biased")
        top_ready = sem("top_ready")
        gap_ready = sem("gap_ready")
        exp_done = sem("exp_done")
        sink_exp_done = sem("sink_exp_done")
        probs_turned = sem("probs_turned")
        probs_copied_a = sem("probs_copied_a")
        probs_copied_v = sem("probs_copied_v")
        attn_mm = sem("attn_mm")
        attn_scaled = sem("attn_scaled")
        gu_tile0 = sem("gu_tile0")
        silu_done = sem("silu_done")
        h_done = sem("h_done")
        h_turned = sem("h_turned")
        ht_hi_done = sem("ht_hi_done")
        ht_lo_done = sem("ht_lo_done")
        tok_hi_done = sem("tok_hi_done")
        tok_lo_done = sem("tok_lo_done")
        router_hi_done = sem("router_hi_done")
        router_lo_done = sem("router_lo_done")
        logits_mm = sem("logits_mm")
        logits_copied = sem("logits_copied")
        logits_turned = sem("logits_turned")
        gap_to_best = sem("gap_to_best")
        weight_exp = sem("weight_exp")
        experts_summed = sem("experts_summed")
        chosen_ready = sem("chosen_ready")
        rank_mm = sem("rank_mm")
        slots_ready = sem("slots_ready")
        onehot_ready = sem("onehot_ready")
        rows_picked = sem("rows_picked")
        picked_copied = sem("picked_copied")
        picked_turned = sem("picked_turned")
        xg_hi_done = sem("xg_hi_done")
        xg_lo_done = sem("xg_lo_done")
        onehot_turned = sem("onehot_turned")
        onehot_t_copied = sem("onehot_t_copied")
        y_hi_done = sem("y_hi_done")
        y_lo_done = sem("y_lo_done")
        scattered = sem("scattered")
        expert_added = sem("expert_added")
        out_stored = sem("out_stored")

        gain_plan = []
        for l in range(DEPTH):
            gain_plan += [(0, l, PRE_MIX), (1, l, ATTN), (2, l, POOL), (0, l, POST_MIX), (1, l, PRE_FFN),
                          (0 if l == DEPTH - 1 else 2, l, POST_FFN)]

        def gain_of(l, n):
            at = next(i for i, g in enumerate(gain_plan) if g[1:] == (l, n))
            s = gain_plan[at][0]
            return s, sum(g[0] == s for g in gain_plan[:at])

        GAIN_BYTES = {ATTN: 32, POOL: 16}

        def gain_level(s, fill):
            fills = [g for g in gain_plan if g[0] == s][:fill + 1]
            return sum(GAIN_BYTES.get(g[2], 16) for g in fills)

        def hidden_id(chunk, t, nt):
            return chunk * TT + t if nt == TT else chunk + (TT - 1) * NCH

        def ffn_steps(eng, first_use, first_chunk, step, tail):
            for c in (0, 1):
                step(c, first_use + c, first_chunk + c)
            with eng.Fori(0, (NCH - 3) // 2) as m:
                for c in (2, 3):
                    step(c, m * 2 + (first_use + c), m * 2 + (first_chunk + c), m)
            step(NCH - 1, first_use + NCH - 1, first_chunk + NCH - 1)
            tail(first_chunk + NCH - 1)

        def static_width(use):
            if use >= use_ffn(1) or use == use_ffn(0):
                return None
            return FC if use in (use_mix(0, 2), use_mix(1, 2)) else 2 * FC

        def next_width(c, nt):
            return 2 * FC if nt == TT and c == NCH - 1 else None

        def piece(parity, h, width):
            if width is None:
                return (slice(None), parity, slice(h * KT // 2, (h + 1) * KT // 2))
            return (slice(None), parity, slice(None), slice(h * width // 2, (h + 1) * width // 2))

        block = ctx.enter_context(nc.Block())

        @block.sync
        def _(sp):
            def free_piece(use, h):
                if not (isinstance(use, int) and use < 2):
                    sp.wait_ge(gu_lo_done, use * 2 + (h - 3))

            def load_mix(l, n):
                u = use_mix(l, n)
                w = w_in[l] if n < W_IN_USES else w_out[l]
                c0 = 2 * FC * (n if n < W_IN_USES else n - W_IN_USES)
                half = min(2 * FC, w.shape[1] - c0) // 2
                for h in range(2):
                    free_piece(u, 1 if n in (0, 1, 4) else h)
                    for k0 in (0, KT // 2):
                        sp.dma_start(raw_gu[:, u % 2, k0:k0 + KT // 2, h * half:(h + 1) * half],
                                     w[k0 * P:(k0 + KT // 2) * P, c0 + h * half:c0 + (h + 1) * half]
                                     .rearrange("(k p) n -> p k n", p=P)).then_inc(gu_loaded[u % 2][h], 16)

            def load_gate_up(w_gate, w_up, use, parity, cols, after_mix=False):
                for h in range(2):
                    free_piece(use, 1 if after_mix else h)
                    k0 = h * KT // 2
                    for n, w in enumerate((w_gate, w_up)):
                        sp.dma_start(raw_gu[:, parity, k0:k0 + KT // 2, n * FC:(n + 1) * FC],
                                     w[k0 * P:(k0 + KT // 2) * P, cols].rearrange("(k p) n -> p k n", p=P)
                                     ).then_inc(gu_loaded[parity][h], 16)

            def free_down(chunk):
                if not (isinstance(chunk, int) and chunk < 2):
                    sp.wait_ge(d_lo_done, chunk * 2 - 2)

            def load_down(w_down, rows_of_chunk, d_parity):
                sp.dma_start(raw_d[:, d_parity, :, :], w_down[rows_of_chunk, :].rearrange("(k p) n -> p k n", p=P)
                             ).then_inc(d_loaded[d_parity], 16)

            def load_network(w_gate, w_up, w_down, use0, parity0, chunk0, d_parity0, load_next, load_after=None):
                def gate_up(c, m=None):
                    c_at = c if m is None else m * 2 + c
                    load_gate_up(w_gate, w_up, use0 + c_at, (parity0 + c) % 2, bass.ds(c_at * FC, FC),
                                 after_mix=c == 1)

                def down(c, m=None):
                    c_at = c if m is None else m * 2 + c
                    if c:
                        free_down(chunk0 + c_at)
                    load_down(w_down, bass.ds(c_at * FC, FC), (d_parity0 + c) % 2)

                free_down(chunk0)
                if load_after is None:
                    gate_up(1)
                for c in (0, 1):
                    down(c)
                    gate_up(c + 2)
                with sp.Fori(0, (NCH - 5) // 2) as m:
                    for c in (2, 3):
                        down(c, m)
                        gate_up(c + 2, m)
                down(NCH - 3)
                gate_up(NCH - 1)
                down(NCH - 2)
                load_next()
                down(NCH - 1)
                if load_after is not None:
                    load_after()

            def load_experts(n_pass):
                def pair(i, last):
                    for half in range(2):
                        e = i * 2 + half
                        use0 = i * (2 * NCH) + (use_ffn(1) + (n_pass * E + half) * NCH)
                        parity0 = (use_ffn(1) + half * NCH) % 2
                        pick = lambda w, n: w[0, bass.ds(n, 1)].rearrange("a k n -> (a k) n")
                        after = 0 if last and half == 1 else e + 1
                        ahead = lambda c: load_gate_up(pick(moe_w_gate, after), pick(moe_w_up, after),
                                                       use0 + (NCH + c), (parity0 + NCH + c) % 2,
                                                       slice(c * FC, (c + 1) * FC))
                        load_network(pick(moe_w_gate, e), pick(moe_w_up, e), pick(moe_w_down, e), use0, parity0,
                                     i * (2 * NCH) + (n_pass * E + half + 1) * NCH, (half + 1) % 2,
                                     lambda: ahead(0), lambda: ahead(1))

                with sp.Fori(0, E // 2 - 1) as i:
                    pair(i, False)
                pair(E // 2 - 1, True)

            for n in range(MIX_USES):
                load_mix(0, n)
            u = use_ffn(0)
            load_gate_up(dense_w_gate[0], dense_w_up[0], u, u % 2, slice(0, FC), after_mix=True)
            load_network(dense_w_gate[0], dense_w_up[0], dense_w_down[0], u, u % 2, 0, 0, lambda: load_mix(1, 0))
            for n in range(1, MIX_USES):
                load_mix(1, n)
            u = use_ffn(1)
            for c in (0, 1):
                load_gate_up(moe_w_gate[0, 0], moe_w_up[0, 0], u + c, (u + c) % 2, slice(c * FC, (c + 1) * FC),
                             after_mix=True)
            load_experts(0)
            sp.wait_ge(slots_ready, 1)
            count = sp.value_load(overflow[0:1, 0:1], min_val=0, max_val=S)
            with sp.If(count > P):
                load_experts(1)
            for t in range(TT):
                sp.wait_ge(x_updated, TT * (2 * DEPTH - 1) + t + 1)
                sp.dma_start(out[0, t * P:(t + 1) * P, :], x_res[:, t, :]).then_inc(out_stored, 16)
            sp.wait_ge(out_stored, 16 * TT)

        @block.gpsimd
        def _(pool):
            pool.memset(ident[:], 0.0).then_inc(const_made, 1)
            pool.memset(eps[:], EPS).then_inc(const_made, 1)
            pool.wait_ge(const_made, 2)
            pool.affine_select(out=ident[:], in_=ident[:], compare_op=ALU.not_equal, fill=1.0, base=0,
                               pattern=[[-1, P]], channel_multiplier=1).then_inc(const_made, 1)
            pool.iota(recip_count[:], pattern=[[0, NG], [1, PAD]], base=1, channel_multiplier=0,
                      allow_small_or_imprecise_dtypes=True).then_inc(const_made, 1)
            pool.dma_start(sinks[:].rearrange("p l h -> p (l h)"),
                           attn_sinks.rearrange("(a l) h -> a (l h)", a=1).broadcast_to([P, DEPTH * N_HEADS])
                           ).then_inc(sinks_loaded, 16)

            def load_gain(n):
                s, l, what = gain_plan[n]
                fill = gain_of(l, what)[1]
                if fill:
                    _, lf, former = [g for g in gain_plan[:n] if g[0] == s][-1]
                    pool.wait_ge(*{PRE_MIX: (rows_ready, tr_id(lf, T_MIX, 1) + 1),
                                   POOL: (pool_scaled, TT * (lf + 1)),
                                   ATTN: (rows_ready, tr_id(lf, T_OUT, 1) + 1),
                                   POST_MIX: (x_updated, TT * (2 * lf + 1)),
                                   PRE_FFN: (rows_ready, tr_id(lf, T_FFN, 1) + 1),
                                   POST_FFN: (x_updated, TT * (2 * lf + 2))}[former])
                wide = lambda g: g[l:l + 1, :].broadcast_to([P, g.shape[1]])
                if what == ATTN:
                    pool.dma_start(gains[s][:, 0:HALF], wide(attn_out_gain)).then_inc(gain_loaded[s], 16)
                    pool.dma_start(gains[s][:, HALF:D], wide(pool_out_gain)).then_inc(gain_loaded[s], 16)
                elif what == POOL:
                    pool.dma_start(gains[s][:, 0:HALF], wide(pool_scale)).then_inc(gain_loaded[s], 16)
                else:
                    g = {PRE_MIX: pre_mix_gain, POST_MIX: post_mix_gain, PRE_FFN: pre_ffn_gain,
                         POST_FFN: post_ffn_gain}[what]
                    pool.dma_start(gains[s][:], wide(g)).then_inc(gain_loaded[s], 16)

            def make_dist():
                for t, c0, n in ((0, 0, P), (1, P, 2 * P)):
                    pool.iota(dist[:, c0:c0 + n], pattern=[[-1, n]], base=t * P, channel_multiplier=1,
                              allow_small_or_imprecise_dtypes=True).then_inc(dist_made, 1)

            def mask_dist(l):
                pool.wait_ge(dist_made, 3 * l + 3)
                hidden_keys = [dist[0:CHUNK, CHUNK:P],
                        dist[0:CHUNK, P:P + CHUNK], dist[0:CHUNK, P + 3 * CHUNK:P + 4 * CHUNK],
                        dist[CHUNK:P, P:P + 2 * CHUNK]]
                for s in hidden_keys:
                    pool.memset(s, FAR).then_inc(masked, 1)

            for n in range(3):
                load_gain(n)
            pool.dma_start(pool_w_sb[:], pool_w[0].rearrange("g c d -> c g d")).then_inc(pool_w_loaded, 16)
            make_dist()
            mask_dist(0)
            for n in range(3, 6):
                load_gain(n)
            pool.wait_ge(pool_mm, TT)
            pool.dma_start(pool_w_sb[:], pool_w[1].rearrange("g c d -> c g d")).then_inc(pool_w_loaded, 16)
            for n in range(6, 9):
                load_gain(n)
            pool.wait_ge(d_used, NCH)
            make_dist()
            mask_dist(1)
            for n in range(9, 12):
                load_gain(n)
            pool.wait_ge(rows_ready, tr_id(1, T_OUT, 1) + 1)
            pool.dma_start(router_raw[:], moe_router[0].rearrange("(k p) e -> p k e", p=P)
                           ).then_inc(router_loaded, 16)
            pool.iota(slot_iota[:], pattern=[[1, P]], base=0, channel_multiplier=0,
                      allow_small_or_imprecise_dtypes=True).then_inc(ffn_const_made, 1)
            pool.memset(ones[:], 1.0).then_inc(ffn_const_made, 1)
            pool.memset(before[:], 1.0).then_inc(ffn_const_made, 1)
            pool.memset(tie[:], 1.0).then_inc(ffn_const_made, 1)
            pool.memset(slot[:], NOT_CHOSEN).then_inc(ffn_const_made, 1)
            pool.wait_ge(ffn_const_made, 5)
            pool.affine_select(out=before[:], in_=before[:], compare_op=ALU.is_gt, fill=0.0, base=0,
                               pattern=[[1, P]], channel_multiplier=-1).then_inc(ffn_const_made, 1)
            pool.affine_select(out=tie[:], in_=tie[:], compare_op=ALU.is_gt, fill=0.0, base=0,
                               pattern=[[1, E], [-1, E]], channel_multiplier=0).then_inc(ffn_const_made, 1)

        @block.scalar
        def _(act):
            for t in range(TT):
                act.dma_start(x_res[:, t, :], x[0, t * P:(t + 1) * P, :]).then_inc(x_loaded[t], 16)

            def split_gu(use, parity, h, level, width=None):
                act.wait_ge(gu_loaded[parity][h], level)
                if not (isinstance(use, int) and use < 2):
                    act.wait_ge(gu_used, use - 1)
                at = piece(parity, h, width)
                act.copy(hi_gu[at], raw_gu[at]).then_inc(gu_hi_done, 1)

            def split_static(use):
                width = static_width(use)
                for h in range(2):
                    split_gu(use, use % 2, h, 32 * (use // 2 + 1), width)

            def norm(idx, src, junk_out, n):
                act.activation(junk_out, src, ACT.Square, accum_out=sum_sq[:, idx:idx + 1]).then_inc(sq_done, 1)
                act.wait_ge(sq_done, idx + 1)
                act.activation(root[:, idx:idx + 1], sum_sq[:, idx:idx + 1], ACT.Sqrt, scale=1.0 / n,
                               bias=eps[:, 0:1]).then_inc(root_done, 1)

            def transposed(l, n):
                for t in range(TT):
                    act.wait_ge(tr_done, tr_id(l, n, t) + 1)
                    act.copy(xt_hi[:, :, t * P:(t + 1) * P],
                             banks(B_Y + 2 * t, 2).rearrange("p (k s) -> p k s", k=KT)).then_inc(xt_hi_done, 1)

            def mixing(l):
                for t in range(TT):
                    if l:
                        act.wait_ge(x_updated, TT * (2 * l - 1) + t + 1)
                    else:
                        act.wait_ge(x_loaded[t], 16)
                    norm(norm_id(l, PRE_MIX, t), x_res[:, t, :], rows[:, t, :], D)
                if l == 0:
                    split_static(0)
                transposed(l, T_MIX)
                split_static(use_mix(l, 1))
                act.wait_ge(gu_used, use_mix(l, 0) + 1)
                act.copy(q_t[:], banks(B_Y, 2).rearrange("p (m s) -> p m s", m=QM)).then_inc(q_copied, 1)
                split_static(use_mix(l, 2))
                act.wait_ge(gu_used, use_mix(l, 1) + 1)
                for g in range(2):
                    for to in range(2):
                        act.copy(k_t[to * 64:(to + 1) * 64, g, :], ps[g * 64:(g + 1) * 64, 0, 0:S]
                                 ).then_inc(kv_copied, 1)
                act.copy(v_rows[:], ps[:, 1, 0:TT * P].rearrange("p (t c) -> p t c", t=TT)).then_inc(kv_copied, 1)
                act.copy(u_t[:, 0:2, PAD:PAD + S], ps[:, B_Y + 2, :].rearrange("p (g s) -> p g s", g=2)
                         ).then_inc(u_copied, 1)
                split_static(use_mix(l, 3))
                act.wait_ge(gu_used, use_mix(l, 2) + 1)
                act.copy(u_t[:, 2:4, PAD:PAD + S], ps[:, B_Y + 3, :].rearrange("p (g s) -> p g s", g=2)
                         ).then_inc(u_copied, 1)
                for t in range(TT):
                    if t:
                        split_static(use_mix(l, 4))
                    nk = (t + 1) * P
                    act.wait_ge(top_ready, TT * l + t + 1)
                    for s in range(N_HEADS):
                        act.activation(scores[:, s, 0:nk], scores[:, s, 0:nk], ACT.Exp,
                                       bias=neg_top[:, t, s:s + 1], scale=HEAD_DIM ** -0.5,
                                       accum_out=denom[:, t, s:s + 1]).then_inc(exp_done, 1)
                    act.wait_ge(gap_ready, TT * l + t + 1)
                    act.activation(sink_exp[:, t, :], sink_gap[:, t, :], ACT.Exp).then_inc(sink_exp_done, 1)
                    act.wait_ge(probs_turned, TT * l + t + 1)
                    b0 = (B_GU, B_Y)[t]
                    act.copy(probs_t[:, 0:4, 0:t + 1, :],
                             banks(b0, t + 1).rearrange("p (h k s) -> p h k s", h=4, k=t + 1)
                             ).then_inc(probs_copied_a, 1)
                for n in (POOL, ATTN):
                    for t in range(TT):
                        if n == POOL:
                            act.wait_ge(pool_scaled, TT * l + t + 1)
                        else:
                            act.wait_ge(attn_scaled, TT * l + t + 1)
                        c0 = HALF if n == POOL else 0
                        norm(norm_id(l, n, t), rows[:, t, c0:c0 + HALF], junk[:], HALF)
                transposed(l, T_OUT)
                split_static(use_ffn(l))
                for t in range(TT):
                    act.wait_ge(gu_used, use_mix(l, 4) + 1)
                    norm(norm_id(l, POST_MIX, t), banks(B_Y + 2 * t, 2), rows[:, t, :], D)
                for t in range(TT):
                    act.wait_ge(x_updated, TT * 2 * l + t + 1)
                    norm(norm_id(l, PRE_FFN, t), x_res[:, t, :], rows[:, t, :], D)
                transposed(l, T_FFN)

            def network(first_use, parity0, use_level, first_chunk, d_level, d_parity0, nt, after_first):
                def split_d(c, chunk, m):
                    b = (d_parity0 + c) % 2
                    act.wait_ge(d_loaded[b], (d_level(c) if m is None else d_level(c) + m * 16))
                    if not (isinstance(chunk, int) and chunk == 0):
                        act.wait_ge(d_used, chunk)
                    for k in range(2):
                        act.copy(hi_d[:, k, :], raw_d[:, b, k, :]).then_inc(d_hi_done, 1)

                def turn(chunk):
                    act.wait_ge(h_turned, chunk + 1)
                    w = nt * P
                    act.copy(ht_hi[:, :, 0:w], ps[:, B_TP, 0:2 * w].rearrange("p (k s) -> p k s", k=2)
                             ).then_inc(ht_hi_done, 1)

                def step(c, use, chunk, m=None):
                    if c > 0:
                        split_d(c - 1, chunk - 1, m)
                    nxt = (parity0 + c + 1) % 2
                    level = use_level(c + 1) if m is None else use_level(c + 1) + m * 32
                    ahead = nt == 1 and c == 0
                    if not ahead:
                        split_gu(use + 1, nxt, 0, level, next_width(c, nt))
                    if c > 0:
                        turn(chunk - 1)
                    if c == 1:
                        after_first()
                    if not ahead:
                        split_gu(use + 1, nxt, 1, level, next_width(c, nt))
                    for t in range(nt):
                        idx = hidden_id(chunk, t, nt)
                        b = t if nt == TT else (h_parity0 + c) % 2
                        if nt == TT and t == 0:
                            act.wait_ge(gu_tile0, chunk + 1)
                        else:
                            act.wait_ge(gu_used, use + 1)
                        if not (isinstance(idx, int) and idx < 2):
                            act.wait_ge(h_done, idx - 1)
                        act.activation(silu[:, b, :], ps[:, B_GU + b, 0:FC], ACT.Silu).then_inc(silu_done, 1)

                h_parity0 = (d_parity0 + NCH) % 2

                def tail(chunk):
                    split_d(NCH - 1, chunk, None)
                    turn(chunk)

                ffn_steps(act, first_use, first_chunk, step, tail)

            def experts(n_pass):
                def copy_picked(number):
                    act.wait_ge(rows_picked, number + 1)
                    act.copy(picked[:], banks(B_Y + 2, 2)).then_inc(picked_copied, 1)

                def xg(number, half):
                    act.wait_ge(picked_turned, number + 1)
                    act.copy(xt_hi[:, :, half * P:(half + 1) * P],
                             banks(B_Y + 2, 2).rearrange("p (k s) -> p k s", k=KT)).then_inc(xg_hi_done, 1)

                copy_picked(n_pass * (E + 1))
                xg(n_pass * (E + 1), 0)
                base = n_pass * E
                with act.Fori(0, E // 2) as i:
                    for half in range(2):
                        e = i * 2 + (base + half)
                        use0 = use_ffn(1) + (base + half) * NCH
                        ch0 = NCH + (base + half) * NCH
                        use_lv = lambda c: i * (32 * NCH) + 32 * ((use0 + c) // 2 + 1)
                        d_lv = lambda c: i * (16 * NCH) + 16 * ((ch0 + c) // 2 + 1)
                        expert_network(i, e, use0, ch0, use_lv, d_lv)
                        following = i * 2 + (n_pass * (E + 1) + half + 1)
                        copy_picked(following)
                        ahead = lambda h: split_gu(i * (2 * NCH) + (use0 + NCH + 1), (use0 + NCH + 1) % 2, h,
                                                   use_lv(NCH + 1))
                        ahead(0)
                        xg(following, 1 - half)
                        act.wait_ge(d_used, i * (2 * NCH) + (ch0 + NCH))
                        act.copy(y_part(xt_hi, half), banks(B_Y, 2).rearrange("p (k s) -> p k s", k=KT)
                                 ).then_inc(y_hi_done, 1)
                        ahead(1)

            def expert_network(i, e, use0, ch0, use_lv, d_lv):
                def copy_onehot_t():
                    act.wait_ge(onehot_turned, e + 1)
                    act.copy(onehot_t[:], ps[:, B_Y + 2, 0:S]).then_inc(onehot_t_copied, 1)

                network(i * (2 * NCH) + use0, use0 % 2, use_lv, i * (2 * NCH) + ch0, d_lv, ch0 % 2, 1, copy_onehot_t)

            act.wait_ge(const_made, 4)
            for l in range(DEPTH):
                mixing(l)
                if l == 0:
                    network(use_ffn(0), use_ffn(0) % 2, lambda c: 32 * ((use_ffn(0) + c) // 2 + 1), 0,
                            lambda c: 16 * (c // 2 + 1), 0, TT, lambda: None)
                    for t in range(TT):
                        act.wait_ge(d_used, NCH)
                        norm(norm_id(0, POST_FFN, t), banks(B_Y + 2 * t, 2), rows[:, t, :], D)
            for t in range(TT):
                act.wait_ge(rows_ready, tr_id(1, T_FFN, t) + 1)
                act.copy(tok_hi[:, t, :], rows[:, t, :]).then_inc(tok_hi_done, 1)
            act.wait_ge(router_loaded, 16)
            act.copy(router_hi[:], router_raw[:]).then_inc(router_hi_done, 1)
            split_static(use_ffn(1) + 1)
            act.wait_ge(gap_to_best, 1)
            act.activation(weight[:], gap[:], ACT.Exp).then_inc(weight_exp, 1)
            experts(0)
            act.wait_ge(slots_ready, 1)
            count = act.value_load(overflow[0:1, 0:1], min_val=0, max_val=S)
            with act.If(count > P):
                experts(1)
            act.wait_ge(experts_summed, 1)
            for t in range(TT):
                norm(norm_id(1, POST_FFN, t), rows[:, t, :], gains[2][:], D)

        @block.tensor
        def _(pe):
            def mm3(o, a_hi, a_lo, b_hi, b_lo, first, last):
                pe.matmul(o, a_hi, b_hi, start=first, stop=False)
                pe.matmul(o, a_hi, b_lo, start=False, stop=False)
                return pe.matmul(o, a_lo, b_hi, start=False, stop=last)

            def turn_rows(l, n):
                for t in range(TT):
                    pe.wait_ge(rows_ready, tr_id(l, n, t) + 1)
                    for k in range(KT):
                        last = pe.transpose(ps[:, B_Y + 2 * t + k // 4, (k % 4) * P:(k % 4 + 1) * P],
                                            rows[:, t, k * P:(k + 1) * P], ident[:])
                    last.then_inc(tr_done, 1)
                pe.wait_ge(xt_lo_done, tr_id(l, n, TT - 1) + 1)

            def rows_times(use, b0):
                for t in range(TT):
                    for k in range(KT):
                        if t == 0 and k == 0:
                            pe.wait_ge(gu_lo_done, 2 * use + 2)
                        a = slice(t * P, (t + 1) * P)
                        last = mm3(ps[:, b0(t), :], xt_hi[:, k, a], xt_lo[:, k, a], hi_gu[:, use % 2, k, :],
                                   lo_gu[:, use % 2, k, :], k == 0, k == KT - 1)
                last.then_inc(gu_used, 1)

            def cols_times(use, c0, o):
                b = use % 2
                for k in range(KT):
                    last = mm3(o, hi_gu[:, b, k, c0:c0 + P], lo_gu[:, b, k, c0:c0 + P], xt_hi[:, k, :],
                               xt_lo[:, k, :], k == 0, k == KT - 1)
                return last

            def mixing(l):
                turn_rows(l, T_MIX)
                u = use_mix(l, 0)
                for m in range(QM):
                    if m % 2 == 0:
                        pe.wait_ge(gu_lo_done, 2 * u + m // 2 + 1)
                    last = cols_times(u, m * P, ps[:, B_Y + m // 2, (m % 2) * S:(m % 2 + 1) * S])
                last.then_inc(gu_used, 1)
                u += 1
                pe.wait_ge(gu_lo_done, 2 * u + 2)
                cols_times(u, 0, ps[:, 0, 0:S])
                for t in range(TT):
                    for k in range(KT):
                        a = slice(t * P, (t + 1) * P)
                        mm3(ps[:, 1, t * P:(t + 1) * P], xt_hi[:, k, a], xt_lo[:, k, a],
                            hi_gu[:, u % 2, k, P:2 * P], lo_gu[:, u % 2, k, P:2 * P], k == 0, k == KT - 1)
                for m in range(2):
                    last = cols_times(u, (2 + m) * P, ps[:, B_Y + 2, m * S:(m + 1) * S])
                last.then_inc(gu_used, 1)
                u += 1
                pe.wait_ge(gu_lo_done, 2 * u + 2)
                for m in range(2):
                    last = cols_times(u, m * P, ps[:, B_Y + 3, m * S:(m + 1) * S])
                last.then_inc(gu_used, 1)

                def score_products(t):
                    nk = (t + 1) * P
                    for h in range(N_HEADS):
                        r, m = h % 2, h // 2
                        rows64 = slice(r * 64, (r + 1) * 64)
                        c0 = (m % 2) * S
                        last = pe.matmul(ps[:, B_Y + 2 * r + m // 2, c0:c0 + nk],
                                         q_t[rows64, m, t * P:(t + 1) * P], k_t[rows64, h // 4, 0:nk],
                                         start=True, stop=True)
                    last.then_inc(scores_mm, 1)

                pe.wait_ge(q_copied, l + 1)
                pe.wait_ge(kv_copied, 5 * (l + 1))
                pe.wait_ge(u_copied, 2 * (l + 1))
                score_products(0)
                pe.wait_ge(pooled_ready, l + 1)
                pe.wait_ge(pool_w_loaded, 16 * (l + 1))
                for t in range(TT):
                    for g in range(NG):
                        last = pe.matmul(ps[:, B_MISC - t, g * P:(g + 1) * P],
                                         u_t[:, g, PAD + t * P:PAD + (t + 1) * P], pool_w_sb[:, g, :],
                                         start=True, stop=True)
                    last.then_inc(pool_mm, 1)
                pe.wait_ge(scores_biased, N_HEADS * (TT * l + 1))
                score_products(1)
                for t in range(TT):
                    pe.wait_ge(exp_done, N_HEADS * (TT * l + t + 1))
                    if t:
                        pe.wait_ge(scores_biased, N_HEADS * (TT * l + t + 1))
                    for s in range(N_HEADS):
                        for kt in range(t + 1):
                            n = s * (t + 1) + kt
                            last = pe.transpose(ps[:, (B_GU, B_Y)[t] + n // 4, (n % 4) * P:(n % 4 + 1) * P],
                                                scores[:, s, kt * P:(kt + 1) * P], ident[:])
                    last.then_inc(probs_turned, 1)
                    pe.wait_ge(pool_scaled, TT * (l + 1))
                    pe.wait_ge(probs_copied_a, TT * l + t + 1)
                    pe.wait_ge(probs_copied_v, TT * l + t + 1)
                    for h in range(N_HEADS):
                        s = (h % 2) * 4 + h // 2
                        kv = slice((h // 4) * HEAD_DIM, (h // 4 + 1) * HEAD_DIM)
                        for kt in range(t + 1):
                            last = pe.matmul(ps[:, B_TP + t, h * HEAD_DIM:(h + 1) * HEAD_DIM],
                                             probs_t[:, s, kt, :], v_rows[:, kt, kv], start=(kt == 0),
                                             stop=(kt == t))
                    last.then_inc(attn_mm, 1)
                turn_rows(l, T_OUT)
                for n in range(W_OUT_USES):
                    rows_times(use_mix(l, W_IN_USES + n), lambda t: B_Y + 2 * t + n)
                turn_rows(l, T_FFN)

            def network(first_use, parity0, first_chunk, h_parity0, nt, x0, before_first_turn, after_first_turn,
                        before_last_turn, before_last_down):
                def gate_up(c, use, chunk, t, before_second):
                    idx = hidden_id(chunk, t, nt)
                    b = t if nt == TT else (h_parity0 + c) % 2
                    w = (parity0 + c) % 2
                    if not (isinstance(idx, int) and idx < 2):
                        pe.wait_ge(h_done, idx - 1)
                    for k in range(KT):
                        if k == KT // 2:
                            before_second()
                        if t == 0 and k % (KT // 2) == 0:
                            pe.wait_ge(gu_lo_done, use * 2 + (1 if k == 0 else 2))
                        a = slice(x0 + t * P, x0 + (t + 1) * P)
                        last = mm3(ps[:, B_GU + b, :], xt_hi[:, k, a], xt_lo[:, k, a], hi_gu[:, w, k, :],
                                   lo_gu[:, w, k, :], k == 0, k == KT - 1)
                    last.then_inc(gu_tile0 if t < nt - 1 else gu_used, 1)

                def turn(c, chunk):
                    if c == 0:
                        before_first_turn()
                    pe.wait_ge(h_done, hidden_id(chunk, nt - 1, nt) + 1)
                    if not (isinstance(chunk, int) and chunk == 0):
                        pe.wait_ge(ht_lo_done, chunk)
                    for t in range(nt):
                        b = t if nt == TT else (h_parity0 + c) % 2
                        for k in range(2):
                            c0 = k * nt * P + t * P
                            last = pe.transpose(ps[:, B_TP, c0:c0 + P], hidden[:, b, k * P:(k + 1) * P], ident[:])
                    last.then_inc(h_turned, 1)
                    if c == 0:
                        after_first_turn()

                def down(c, chunk):
                    pe.wait_ge(ht_lo_done, chunk + 1)
                    for k in range(2):
                        pe.wait_ge(d_lo_done, chunk * 2 + (k + 1))
                        for t in range(nt):
                            a = slice(t * P, (t + 1) * P)
                            for n in range(2):
                                cols = slice(n * 512, (n + 1) * 512)
                                last = mm3(ps[:, B_Y + 2 * t + n, :], ht_hi[:, k, a], ht_lo[:, k, a],
                                           hi_d[:, k, cols], lo_d[:, k, cols], c == 0 and k == 0,
                                           c == NCH - 1 and k == 1)
                    last.then_inc(d_used, 1)

                def step(c, use, chunk, m=None):
                    turn_prev = (lambda: turn(c - 1, chunk - 1)) if c else (lambda: None)
                    gate_up(c, use, chunk, 0, turn_prev)
                    if nt == TT:
                        gate_up(c, use, chunk, 1, lambda: None)
                    if c:
                        down(c - 1, chunk - 1)

                def tail(chunk):
                    before_last_turn()
                    turn(NCH - 1, chunk)
                    before_last_down()
                    down(NCH - 1, chunk)

                ffn_steps(pe, first_use, first_chunk, step, tail)

            def pick_rows(number):
                pe.wait_ge(onehot_ready, number + 1)
                for t in range(TT):
                    for part in (tok_hi, tok_lo):
                        for n in range(2):
                            last = pe.matmul(ps[:, B_Y + 2 + n, :], onehot[:, t, :],
                                             part[:, t, n * 512:(n + 1) * 512], start=(t == 0 and part is tok_hi),
                                             stop=(t == TT - 1 and part is tok_lo))
                last.then_inc(rows_picked, 1)

            def turn_picked(number):
                pe.wait_ge(picked_copied, number + 1)
                for k in range(KT):
                    last = pe.transpose(ps[:, B_Y + 2 + k // 4, (k % 4) * P:(k % 4 + 1) * P],
                                        picked[:, k * P:(k + 1) * P], ident[:])
                last.then_inc(picked_turned, 1)

            def experts(n_pass):
                base = n_pass * E
                g0 = n_pass * (E + 1)
                pick_rows(g0)
                turn_picked(g0)
                with pe.Fori(0, E // 2) as i:
                    for half in range(2):
                        e = i * 2 + (base + half)
                        pe.wait_ge(xg_hi_done, i * 2 + (g0 + half + 1))
                        pe.wait_ge(xg_lo_done, i * 2 + (g0 + half + 1))

                        def rows_added():
                            pe.wait_ge(expert_added, e * TT + 1)

                        def turn_onehot():
                            for t in range(TT):
                                last = pe.transpose(ps[:, B_Y + 2, t * P:(t + 1) * P],
                                                    onehot[:, t, :].bitcast(F32), ident[:])
                            last.then_inc(onehot_turned, 1)

                        def pick_next():
                            pe.wait_ge(onehot_t_copied, e + 1)
                            pick_rows(i * 2 + (g0 + half + 1))

                        def turn_next():
                            turn_picked(i * 2 + (g0 + half + 1))

                        use0 = use_ffn(1) + (base + half) * NCH
                        ch0 = NCH + (base + half) * NCH
                        network(i * (2 * NCH) + use0, use0 % 2, i * (2 * NCH) + ch0, (ch0 + NCH) % 2, 1, half * P,
                                rows_added, turn_onehot, pick_next, turn_next)
                        pe.wait_ge(y_lo_done, e + 1)
                        for t in range(TT):
                            if t == 1:
                                pe.wait_ge(xg_lo_done, i * 2 + (g0 + half + 2))
                            for n in range(2):
                                o = ps[:, (B_TP, B_Y + 2)[t] + n, :]
                                picks = onehot_t[:, t * P:(t + 1) * P]
                                ks = slice(n * KT // 2, (n + 1) * KT // 2)
                                pe.matmul(o, picks, y_part(xt_hi, half)[:, ks, :], start=True, stop=False)
                                last = pe.matmul(o, picks, y_part(xt_lo, half)[:, ks, :], start=False, stop=True)
                            last.then_inc(scattered, 1)

            pe.wait_ge(const_made, 4)
            for l in range(DEPTH):
                mixing(l)
                if l == 0:
                    network(use_ffn(0), use_ffn(0) % 2, 0, 0, TT, 0, *(4 * [lambda: None]))
            pe.wait_ge(router_lo_done, 1)
            o = ps[0:E, B_MISC, 0:S]
            for k in range(KT):
                mm3(o, router_hi[:, k, :], router_lo[:, k, :], xt_hi[:, k, :], xt_lo[:, k, :], k == 0, False)
                last = pe.matmul(o, router_lo[:, k, :], xt_lo[:, k, :], start=False, stop=(k == KT - 1))
            last.then_inc(logits_mm, 1)
            pe.wait_ge(logits_copied, 1)
            for t in range(TT):
                last = pe.transpose(ps[:, B_MISC, t * E:(t + 1) * E], logits_t[:, t * P:(t + 1) * P],
                                    ident[0:E, 0:E])
            last.then_inc(logits_turned, 1)
            pe.wait_ge(chosen_ready, 1)
            pe.wait_ge(ffn_const_made, 7)
            at = lambda n: ps[:, B_MISC, (4 + n) * E:(5 + n) * E]
            pe.matmul(at(0), before[:], chosen[:, 0, :], start=True, stop=True)
            pe.matmul(at(1), ones[:], chosen[:, 0, :], start=True, stop=False)
            pe.matmul(at(1), before[:], chosen[:, 1, :], start=False, stop=True)
            pe.matmul(at(2), ones[:], chosen[:, 0, :], start=True, stop=False)
            pe.matmul(at(2), ones[:], chosen[:, 1, :], start=False, stop=True).then_inc(rank_mm, 1)
            pe.wait_ge(tok_lo_done, TT)
            experts(0)
            pe.wait_ge(slots_ready, 1)
            count = pe.value_load(overflow[0:1, 0:1], min_val=0, max_val=S)
            with pe.If(count > P):
                experts(1)

        @block.vector
        def _(dve):
            steps = [0]

            def link(ins):
                steps[0] += 1
                ins.then_inc(vec_step, 1)
                dve.wait_ge(vec_step, steps[0])

            def split_gu(use, parity, h, width=None):
                dve.wait_ge(gu_hi_done, use * 2 + (h + 1))
                at = piece(parity, h, width)
                dve.tensor_tensor(lo_gu[at], raw_gu[at], hi_gu[at].bitcast(F32), ALU.subtract
                                  ).then_inc(gu_lo_done, 1)

            def split_static(use):
                width = static_width(use)
                for p in range(2):
                    split_gu(use, use % 2, p, width)

            def scale_of(idx):
                dve.wait_ge(root_done, idx + 1)
                dve.reciprocal(rstd[:, idx:idx + 1], root[:, idx:idx + 1]).then_inc(rstd_done, 1)
                dve.wait_ge(rstd_done, idx + 1)
                return rstd[:, idx:idx + 1]

            def low_parts(l, tr):
                for t in range(TT):
                    dve.wait_ge(xt_hi_done, tr_id(l, tr, t) + 1)
                    dve.tensor_tensor(xt_lo[:, :, t * P:(t + 1) * P],
                                      banks(B_Y + 2 * t, 2).rearrange("p (k s) -> p k s", k=KT),
                                      xt_hi[:, :, t * P:(t + 1) * P].bitcast(F32), ALU.subtract
                                      ).then_inc(xt_lo_done, 1)

            def pre_norm(l, n):
                s, fill = gain_of(l, n)
                for t in range(TT):
                    r = scale_of(norm_id(l, n, t))
                    dve.wait_ge(gain_loaded[s], gain_level(s, fill))
                    dve.scalar_tensor_tensor(rows[:, t, :], x_res[:, t, :], r, gains[s][:], ALU.mult, ALU.mult
                                             ).then_inc(rows_ready, 1)

            def post_norm(l, n, src):
                s, fill = gain_of(l, n)
                for t in range(TT):
                    r = scale_of(norm_id(l, n, t))
                    dve.wait_ge(gain_loaded[s], gain_level(s, fill))
                    link(dve.scalar_tensor_tensor(rows[:, t, :], src(t), r, gains[s][:], ALU.mult, ALU.mult))
                    dve.tensor_tensor(x_res[:, t, :], x_res[:, t, :], rows[:, t, :], ALU.add).then_inc(x_updated, 1)

            def pooling(l):
                link(dve.memset(u_t[:, :, 0:PAD], 0.0))
                dve.wait_ge(u_copied, 2 * (l + 1))
                a, b = sums
                W = PAD + S
                src, dst = u_t, a
                for g in range(NG):
                    w = 1 << g
                    lo = 2 * w - 1
                    link(dve.tensor_tensor(dst[:, g:NG, lo:W], src[:, g:NG, lo:W], src[:, g:NG, lo - w:W - w],
                                           ALU.add))
                    src, dst = dst, (b if dst is a else a)
                for g, w in enumerate(POOL_WINDOWS):
                    s = (a, b)[g % 2]
                    link(dve.tensor_tensor(edge[:, g, :], s[:, g, PAD:2 * PAD], recip_count[:, g, :], ALU.mult))
                    link(dve.tensor_tensor(u_t[:, g, PAD:2 * PAD], edge[:, g, :], u_t[:, g, PAD:2 * PAD],
                                           ALU.subtract))
                    last = dve.scalar_tensor_tensor(u_t[:, g, 2 * PAD:W], s[:, g, 2 * PAD:W], 1.0 / w,
                                                    u_t[:, g, 2 * PAD:W], ALU.mult, ALU.subtract)
                    if g < NG - 1:
                        link(last)
                last.then_inc(pooled_ready, 1)

            def attention_scores(l, t):
                nk = (t + 1) * P
                d0 = (0, P)[t]
                dve.wait_ge(scores_mm, TT * l + t + 1)
                dve.wait_ge(masked, 4 * (l + 1))
                dve.wait_ge(sinks_loaded, 16)
                if t:
                    dve.wait_ge(probs_turned, TT * l + t)
                for s in range(N_HEADS):
                    h = (s % 4) * 2 + s // 4
                    slope = 2.0 ** (-8.0 * (h + 1) / N_HEADS)
                    dve.scalar_tensor_tensor(scores[:, s, 0:nk], dist[:, d0:d0 + nk],
                                             -slope * HEAD_DIM ** 0.5,
                                             ps[:, B_Y + s // 2, (s % 2) * S:(s % 2) * S + nk],
                                             ALU.mult, ALU.add).then_inc(scores_biased, 1)
                dve.wait_ge(scores_biased, N_HEADS * (TT * l + t + 1))
                link(dve.tensor_reduce(row_max[:, t, :], scores[:, :, 0:nk], AX.X, ALU.max))
                sink = sinks[:, l, :].rearrange("p (m r) -> p r m", r=2)
                by = lambda x: x[:, t, :].rearrange("p (r m) -> p r m", r=2)
                link(dve.scalar_tensor_tensor(by(top), by(row_max), HEAD_DIM ** -0.5, sink, ALU.mult, ALU.max))
                dve.tensor_scalar(neg_top[:, t, :], top[:, t, :], -1.0, None, ALU.mult).then_inc(top_ready, 1)
                dve.tensor_tensor(by(sink_gap), sink, by(top), ALU.subtract).then_inc(gap_ready, 1)

            def attention_probs(l, t):
                dve.wait_ge(sink_exp_done, TT * l + t + 1)
                link(dve.tensor_tensor(denom_all[:, t, :], denom[:, t, :], sink_exp[:, t, :], ALU.add))
                link(dve.reciprocal(inv_denom[:, t, :], denom_all[:, t, :]))
                dve.wait_ge(probs_turned, TT * l + t + 1)
                b0 = (B_GU, B_Y)[t] + t + 1
                if t:
                    dve.wait_ge(attn_mm, TT * l + t)
                dve.tensor_copy(probs_t[:, 4:8, 0:t + 1, :],
                                banks(b0, t + 1).rearrange("p (h k s) -> p h k s", h=4, k=t + 1)
                                ).then_inc(probs_copied_v, 1)

            def attention_out(l, t):
                dve.wait_ge(attn_mm, TT * l + t + 1)
                dve.tensor_tensor(rows[:, t, 0:HALF].rearrange("p (m r d) -> p m r d", r=2, d=HEAD_DIM),
                                  ps[:, B_TP + t, :].rearrange("p (m r d) -> p m r d", r=2, d=HEAD_DIM),
                                  inv_denom[:, t, :].rearrange("p (r m a) -> p m r a", r=2, a=1)
                                  .broadcast_to([P, 4, 2, HEAD_DIM]), ALU.mult).then_inc(attn_scaled, 1)

            def mixing(l):
                pre_norm(l, PRE_MIX)
                if l == 0:
                    split_static(0)
                low_parts(l, T_MIX)
                dve.wait_ge(dist_made, 3 * l + 2)
                dve.scalar_tensor_tensor(dist[:], dist[:], -1.0, dist[:], ALU.mult, ALU.max).then_inc(dist_made, 1)
                for n in (1, 2):
                    split_static(use_mix(l, n))
                pooling(l)
                attention_scores(l, 0)
                split_static(use_mix(l, 3))
                s, fill = gain_of(l, POOL)
                dve.wait_ge(gain_loaded[s], gain_level(s, fill))
                for t in range(TT):
                    dve.wait_ge(pool_mm, TT * l + t + 1)
                    dve.tensor_tensor(rows[:, t, HALF:D], ps[:, B_MISC - t, :], gains[s][:, 0:HALF], ALU.mult
                                      ).then_inc(pool_scaled, 1)
                attention_probs(l, 0)
                attention_scores(l, 1)
                attention_out(l, 0)
                split_static(use_mix(l, 4))
                attention_probs(l, 1)
                s, fill = gain_of(l, ATTN)
                dve.wait_ge(gain_loaded[s], gain_level(s, fill))
                for n, c0 in ((POOL, HALF), (ATTN, 0)):
                    for t in range(TT):
                        if n == ATTN and t == 1:
                            attention_out(l, 1)
                        r = scale_of(norm_id(l, n, t))
                        ins = dve.scalar_tensor_tensor(rows[:, t, c0:c0 + HALF], rows[:, t, c0:c0 + HALF], r,
                                                       gains[s][:, c0:c0 + HALF], ALU.mult, ALU.mult)
                        if n == ATTN:
                            ins.then_inc(rows_ready, 1)
                        else:
                            link(ins)
                low_parts(l, T_OUT)
                split_static(use_ffn(l))
                post_norm(l, POST_MIX, lambda t: banks(B_Y + 2 * t, 2))
                pre_norm(l, PRE_FFN)
                low_parts(l, T_FFN)

            def network(first_use, parity0, first_chunk, d_parity0, nt, before_last):
                def split_d(c, chunk):
                    b = (d_parity0 + c) % 2
                    for k in range(2):
                        dve.wait_ge(d_hi_done, chunk * 2 + (k + 1))
                        dve.tensor_tensor(lo_d[:, k, :], raw_d[:, b, k, :], hi_d[:, k, :].bitcast(F32), ALU.subtract
                                          ).then_inc(d_lo_done, 1)

                def turn(chunk):
                    w = nt * P
                    dve.wait_ge(ht_hi_done, chunk + 1)
                    dve.tensor_tensor(ht_lo[:, :, 0:w], ps[:, B_TP, 0:2 * w].rearrange("p (k s) -> p k s", k=2),
                                      ht_hi[:, :, 0:w].bitcast(F32), ALU.subtract).then_inc(ht_lo_done, 1)

                h_parity0 = (d_parity0 + NCH) % 2

                def step(c, use, chunk, m=None):
                    nxt = (parity0 + c + 1) % 2
                    if c == NCH - 1:
                        before_last()
                    if c > 0:
                        split_d(c - 1, chunk - 1)
                        turn(chunk - 1)
                    ahead = nt == 1 and c == 0
                    if not ahead:
                        split_gu(use + 1, nxt, 0, next_width(c, nt))
                    for t in range(nt):
                        b = t if nt == TT else (h_parity0 + c) % 2
                        dve.wait_ge(silu_done, hidden_id(chunk, t, nt) + 1)
                        dve.tensor_tensor(hidden[:, b, :], silu[:, b, :], ps[:, B_GU + b, FC:2 * FC], ALU.mult
                                          ).then_inc(h_done, 1)
                    if not ahead:
                        split_gu(use + 1, nxt, 1, next_width(c, nt))

                def tail(chunk):
                    split_d(NCH - 1, chunk)
                    turn(chunk)

                ffn_steps(dve, first_use, first_chunk, step, tail)

            def choose():
                dve.wait_ge(logits_mm, 1)
                dve.tensor_copy(logits_t[:], ps[0:E, B_MISC, 0:S]).then_inc(logits_copied, 1)
                dve.wait_ge(logits_turned, 1)
                dve.wait_ge(ffn_const_made, 7)
                link(dve.tensor_copy(logits[:], ps[:, B_MISC, 0:TT * E].rearrange("p (t e) -> p t e", t=TT)))
                link(dve.tensor_reduce(best[:], logits[:], AX.X, ALU.max))
                wide = lambda x: x[:].rearrange("p (t a) -> p t a", a=1).broadcast_to([P, TT, E])
                dve.tensor_tensor(gap[:], logits[:], wide(best), ALU.subtract).then_inc(gap_to_best, 1)
                for t in range(TT):
                    other = logits[:, t, :].rearrange("p (a e) -> p a e", a=1).broadcast_to([P, E, E])
                    own = logits[:, t, :].rearrange("p (e a) -> p e a", a=1).broadcast_to([P, E, E])
                    link(dve.tensor_tensor(beats[:], other, own, ALU.is_gt))
                    link(dve.tensor_tensor(ties[:], other, own, ALU.is_equal))
                    link(dve.tensor_tensor(ties[:], ties[:], tie[:], ALU.mult))
                    link(dve.tensor_tensor(beats[:], beats[:], ties[:], ALU.add))
                    link(dve.tensor_reduce(rank[:, t, :], beats[:], AX.X, ALU.add))
                dve.tensor_scalar(chosen[:], rank[:], 1.5, None, ALU.is_lt).then_inc(chosen_ready, 1)
                dve.wait_ge(chosen_ready, 1)
                dve.wait_ge(weight_exp, 1)
                link(dve.tensor_tensor(weight[:], weight[:], chosen[:], ALU.mult))
                link(dve.tensor_reduce(weight_sum[:], weight[:], AX.X, ALU.add))
                link(dve.reciprocal(best[:], weight_sum[:]))
                link(dve.tensor_tensor(gates[:], weight[:], wide(best), ALU.mult))
                dve.wait_ge(rank_mm, 1)
                link(dve.scalar_tensor_tensor(rank[:], ps[:, B_MISC, 4 * E:6 * E].rearrange("p (t e) -> p t e", t=TT),
                                              -NOT_CHOSEN, chosen[:], ALU.add, ALU.mult))
                link(dve.tensor_scalar(slot[:, 0, :, 0:E], rank[:], NOT_CHOSEN, None, ALU.add))
                link(dve.tensor_scalar(slot[:, 1, :, 0:E], slot[:, 0, :, 0:E], -float(P), None, ALU.add))
                link(dve.tensor_reduce(most[0:1, 0:1], ps[0:1, B_MISC, 6 * E:7 * E], AX.X, ALU.max))
                dve.tensor_copy(overflow[0:1, 0:1], most[0:1, 0:1]).then_inc(slots_ready, 1)
                dve.wait_ge(slots_ready, 1)

            def experts(n_pass):
                base = n_pass * E
                g0 = n_pass * (E + 1)

                def make_onehot(number, expert):
                    for t in range(TT):
                        last = dve.tensor_scalar(onehot[:, t, :], slot_iota[:], slot[:, n_pass, t, expert], None,
                                                 ALU.is_equal)
                    last.then_inc(onehot_ready, 1)

                def gathered(number, half):
                    dve.wait_ge(xg_hi_done, number + 1)
                    dve.tensor_tensor(xt_lo[:, :, half * P:(half + 1) * P],
                                      banks(B_Y + 2, 2).rearrange("p (k s) -> p k s", k=KT),
                                      xt_hi[:, :, half * P:(half + 1) * P].bitcast(F32), ALU.subtract
                                      ).then_inc(xg_lo_done, 1)

                if n_pass:
                    dve.wait_ge(rows_picked, g0)
                make_onehot(g0, slice(0, 1))
                gathered(g0, 0)
                with dve.Fori(0, E // 2) as i:
                    for half in range(2):
                        e = i * 2 + (base + half)
                        use0 = use_ffn(1) + (base + half) * NCH
                        ch0 = NCH + (base + half) * NCH

                        def next_onehot():
                            dve.wait_ge(onehot_turned, e + 1)
                            make_onehot(i * 2 + (g0 + half + 1), bass.ds(i * 2 + (half + 1), 1))

                        network(i * (2 * NCH) + use0, use0 % 2, i * (2 * NCH) + ch0, ch0 % 2, 1, next_onehot)
                        ahead = lambda h: split_gu(i * (2 * NCH) + (use0 + NCH + 1), (use0 + NCH + 1) % 2, h)
                        ahead(0)
                        gathered(i * 2 + (g0 + half + 1), 1 - half)
                        dve.wait_ge(y_hi_done, e + 1)
                        dve.tensor_tensor(y_part(xt_lo, half), banks(B_Y, 2).rearrange("p (k s) -> p k s", k=KT),
                                          y_part(xt_hi, half).bitcast(F32), ALU.subtract).then_inc(y_lo_done, 1)
                        ahead(1)
                        for t in range(TT):
                            dve.wait_ge(scattered, e * TT + (t + 1))
                            dve.wait_ge(expert_added, e * TT + 1)
                            dve.scalar_tensor_tensor(rows[:, t, :], banks((B_TP, B_Y + 2)[t], 2),
                                                     gates[:, t, bass.ds(i * 2 + half, 1)], rows[:, t, :],
                                                     ALU.mult, ALU.add).then_inc(expert_added, 1)
                dve.wait_ge(expert_added, TT * (base + E) + 1)

            dve.wait_ge(const_made, 4)
            for g, w in enumerate(POOL_WINDOWS):
                link(dve.tensor_scalar(recip_count[:, g, :], recip_count[:, g, :], float(w), None, ALU.min))
            link(dve.reciprocal(recip_count[:], recip_count[:]))
            for l in range(DEPTH):
                mixing(l)
                if l == 0:
                    network(use_ffn(0), use_ffn(0) % 2, 0, 0, TT, lambda: None)
                    post_norm(0, POST_FFN, lambda t: banks(B_Y + 2 * t, 2))
            dve.wait_ge(router_hi_done, 1)
            dve.tensor_tensor(router_lo[:], router_raw[:], router_hi[:].bitcast(F32), ALU.subtract
                              ).then_inc(router_lo_done, 1)
            for t in range(TT):
                dve.wait_ge(tok_hi_done, t + 1)
                dve.tensor_tensor(tok_lo[:, t, :], rows[:, t, :], tok_hi[:, t, :].bitcast(F32), ALU.subtract
                                  ).then_inc(tok_lo_done, 1)
            dve.wait_ge(tok_lo_done, TT)
            dve.memset(rows[:], 0.0).then_inc(expert_added, 1)
            split_static(use_ffn(1) + 1)
            choose()
            experts(0)
            count = dve.value_load(overflow[0:1, 0:1], min_val=0, max_val=S)
            with dve.If(count > P):
                experts(1)
            dve.memset(most[0:1, 1:2], 0.0).then_inc(experts_summed, 1)
            post_norm(1, POST_FFN, lambda t: rows[:, t, :])


_INS = ["x", "pre_mix_gain", "w_in", "attn_sinks", "pool_w", "pool_scale", "attn_out_gain", "pool_out_gain", "w_out",
        "post_mix_gain", "pre_ffn_gain", "post_ffn_gain", "dense_w_gate", "dense_w_up", "dense_w_down",
        "moe_router", "moe_w_gate", "moe_w_up", "moe_w_down"]


def kernel(**inputs):
    import numpy as np
    import concourse.bacc as bacc
    from concourse.bass_utils import run_bass_kernel_spmd

    nc = bacc.Bacc("TRN2", target_bir_lowering=False, num_devices=1)
    arrays, args = {}, []
    for name in _INS:
        a = np.ascontiguousarray(inputs[name])
        arrays[f"in_{name}"] = a
        args.append(nc.dram_tensor(f"in_{name}", a.shape, mybir.dt.from_np(a.dtype), kind="ExternalInput").ap())
    out = nc.dram_tensor("out_0", arrays["in_x"].shape, F32, kind="ExternalOutput").ap()
    build_trunk(nc, *args, out)
    r = run_bass_kernel_spmd(nc, [arrays], core_ids=[0])
    return r.results[0]["out_0"]
```
